# Optimizing a Trainium2 kernel written in Bass

```python
import math
import jax, jax.numpy as jnp
from jax import lax
import numpy as np

D_MODEL = 1024
BATCH = 1
SEQ = 256
DEPTH = 2
DEC_BATCH = 8
DEC_SEQ = 1
PAST_LEN = 2048
PAGE_SIZE = 128

SSD_EXPAND = 2
D_INNER = SSD_EXPAND * D_MODEL
SSD_HEADDIM = 64
SSD_HEADS = D_INNER // SSD_HEADDIM
SSD_GROUPS = 4
HEADS_PER_GROUP = SSD_HEADS // SSD_GROUPS
D_STATE = 128
CONV_W = 4
CONV_DIM = D_INNER + 2 * SSD_GROUPS * D_STATE
SSD_CHUNK = 128
D_SGU = 2 * D_MODEL
SGU_HEADS = 8
SGU_HEAD_DIM = D_SGU // SGU_HEADS
SGU_CHUNK = 128
D_FF_DENSE = 2816
N_EXPERTS = 8
TOP_K = 2
D_FF_EXPERT = 3584
N_SSD = (DEPTH + 1) // 2
N_SGU = DEPTH // 2
EPS = 1e-5

kernel_name = "hybrid_ssd_chunkmlp_moe_decode_step"

def rmsnorm(x, g):
    xf = x.astype(jnp.float32)
    y = xf * lax.rsqrt(jnp.mean(xf * xf, axis=-1, keepdims=True) + EPS)
    return (y * g.astype(jnp.float32)).astype(x.dtype)

def layernorm(x, g, b):
    xf = x.astype(jnp.float32)
    mu = jnp.mean(xf, axis=-1, keepdims=True)
    var = jnp.mean(jnp.square(xf - mu), axis=-1, keepdims=True)
    y = (xf - mu) * lax.rsqrt(var + EPS) * g.astype(jnp.float32) + b.astype(jnp.float32)
    return y.astype(x.dtype)

def causal_dwconv(xpad, w, b, length):
    out = b + sum(xpad[:, k:k + length] * w[k] for k in range(CONV_W))
    return out

def ssd_chunked(x, dt, a_neg, Bm, Cm):
    b, l = x.shape[:2]
    nc = l // SSD_CHUNK
    q = SSD_CHUNK
    xc = x.reshape(b, nc, q, SSD_GROUPS, HEADS_PER_GROUP, SSD_HEADDIM)
    dtc = dt.reshape(b, nc, q, SSD_GROUPS, HEADS_PER_GROUP)
    Bc = Bm.reshape(b, nc, q, SSD_GROUPS, D_STATE)
    Cc = Cm.reshape(b, nc, q, SSD_GROUPS, D_STATE)
    la_cs = jnp.cumsum(dtc * a_neg.reshape(SSD_GROUPS, HEADS_PER_GROUP), axis=2)
    xdt = xc * dtc[..., None]
    seg = la_cs[:, :, :, None] - la_cs[:, :, None, :]
    causal = jnp.tril(jnp.ones((q, q), dtype=bool))[:, :, None, None]
    decay = jnp.exp(jnp.where(causal, seg, -jnp.inf))
    cb = jnp.einsum('bcign,bcjgn->bcijg', Cc, Bc)
    y_diag = jnp.einsum('bcijgr,bcjgrp->bcigrp', cb[..., None] * decay, xdt)
    decay_to_end = jnp.exp(la_cs[:, :, -1:] - la_cs)
    chunk_states = jnp.einsum('bcjgn,bcjgrp->bcgrpn', Bc, xdt * decay_to_end[..., None])
    chunk_decay = jnp.exp(la_cs[:, :, -1])

    def step(hs, inp):
        st, dec = inp
        return dec[..., None, None] * hs + st, hs

    h0 = jnp.zeros((b, SSD_GROUPS, HEADS_PER_GROUP, SSD_HEADDIM, D_STATE), jnp.float32)
    h_final, h_prev = lax.scan(step, h0, (jnp.moveaxis(chunk_states, 1, 0).astype(jnp.float32),
                                          jnp.moveaxis(chunk_decay, 1, 0)))
    h_prev = jnp.moveaxis(h_prev, 0, 1)
    y_off = jnp.einsum('bcign,bcgrpn->bcigrp', Cc, h_prev) * jnp.exp(la_cs)[..., None]
    y = (y_diag + y_off).reshape(b, l, SSD_HEADS, SSD_HEADDIM)
    return y, h_final.reshape(b, SSD_HEADS, SSD_HEADDIM, D_STATE)

def ssd_recurrent(x, dt, a_neg, Bm, Cm, h0):
    b, l = x.shape[:2]
    xs = x.reshape(b, l, SSD_GROUPS, HEADS_PER_GROUP, SSD_HEADDIM)
    dts = dt.reshape(b, l, SSD_GROUPS, HEADS_PER_GROUP)
    a = a_neg.reshape(SSD_GROUPS, HEADS_PER_GROUP)
    hs0 = h0.reshape(b, SSD_GROUPS, HEADS_PER_GROUP, SSD_HEADDIM, D_STATE).astype(jnp.float32)

    def step(hs, inp):
        xt, dtt, bt, ct = inp
        upd = jnp.einsum('bgn,bgrp->bgrpn', bt, xt * dtt[..., None])
        hs = (jnp.exp(dtt * a)[..., None, None] * hs + upd).astype(jnp.float32)
        yt = jnp.einsum('bgn,bgrpn->bgrp', ct, hs)
        return hs, yt

    tmajor = lambda t: jnp.moveaxis(t, 1, 0)
    h_final, ys = lax.scan(step, hs0, (tmajor(xs), tmajor(dts), tmajor(Bm), tmajor(Cm)))
    y = jnp.moveaxis(ys, 0, 1).reshape(b, l, SSD_HEADS, SSD_HEADDIM)
    return y, h_final.reshape(b, SSD_HEADS, SSD_HEADDIM, D_STATE)

def ssd_mixer(h, conv_prev, ssm_prev, w_in, conv_w, conv_b, dt_bias, a_log, d_skip, gnorm_w, w_out):
    b, L, _ = h.shape
    proj = h @ w_in
    z = proj[..., :D_INNER]
    xbc = proj[..., D_INNER:D_INNER + CONV_DIM]
    dt_raw = proj[..., D_INNER + CONV_DIM:]
    if conv_prev is None:
        conv_prev = jnp.zeros((b, CONV_W - 1, CONV_DIM), xbc.dtype)
    xpad = jnp.concatenate([conv_prev.astype(xbc.dtype), xbc], axis=1)
    new_conv = xpad[:, -(CONV_W - 1):]
    xbc = jax.nn.silu(causal_dwconv(xpad, conv_w, conv_b, L))
    xs = xbc[..., :D_INNER].reshape(b, L, SSD_HEADS, SSD_HEADDIM)
    Bm = xbc[..., D_INNER:D_INNER + SSD_GROUPS * D_STATE].reshape(b, L, SSD_GROUPS, D_STATE)
    Cm = xbc[..., D_INNER + SSD_GROUPS * D_STATE:].reshape(b, L, SSD_GROUPS, D_STATE)
    dt = jax.nn.softplus(dt_raw.astype(jnp.float32) + dt_bias.astype(jnp.float32))
    a_neg = -jnp.exp(a_log.astype(jnp.float32))
    if ssm_prev is None:
        y, new_ssm = ssd_chunked(xs, dt, a_neg, Bm, Cm)
    else:
        y, new_ssm = ssd_recurrent(xs, dt, a_neg, Bm, Cm, ssm_prev)
    y = y + d_skip.astype(jnp.float32)[:, None] * xs.astype(jnp.float32)
    yg = y.reshape(b, L, D_INNER) * jax.nn.silu(z.astype(jnp.float32))
    yg = yg.reshape(b, L, SSD_GROUPS, D_INNER // SSD_GROUPS)
    yg = yg * lax.rsqrt(jnp.mean(yg * yg, axis=-1, keepdims=True) + EPS)
    yg = yg.reshape(b, L, D_INNER) * gnorm_w.astype(jnp.float32)
    return (yg.astype(h.dtype) @ w_out).astype(h.dtype), new_ssm, new_conv

def sgu_mixer(h, w_in, b_in, ln_g, ln_b, w_s, b_s, w_out):
    b, L, _ = h.shape
    uv = jax.nn.gelu(h @ w_in + b_in, approximate=False)
    u, v = uv[..., :D_SGU], uv[..., D_SGU:]
    v = layernorm(v, ln_g, ln_b)
    q = min(L, SGU_CHUNK)
    nc = L // q
    vc = v.reshape(b, nc, q, SGU_HEADS, SGU_HEAD_DIM)
    ws = jnp.tril(w_s[:, :q, :q])
    s = jnp.einsum('gij,bcjgd->bcigd', ws, vc) + jnp.transpose(b_s[:, :q])[None, None, :, :, None]
    y = u * s.reshape(b, L, D_SGU).astype(u.dtype)
    return (y @ w_out).astype(h.dtype), v

def swiglu(h, w_gu, w_down, d_ff):
    gu = h @ w_gu
    return (jax.nn.silu(gu[..., :d_ff]) * gu[..., d_ff:]) @ w_down

def moe_swiglu(h, w_router, w_gu, w_down):
    logits = (h @ w_router).astype(jnp.float32)
    top_v, top_i = lax.top_k(logits, TOP_K)
    gates = jax.nn.softmax(top_v, axis=-1)
    combine = jnp.sum(jax.nn.one_hot(top_i, N_EXPERTS, dtype=jnp.float32) * gates[..., None], axis=-2)
    out = jnp.zeros(h.shape, jnp.float32)
    for e in range(N_EXPERTS):
        out = out + combine[..., e:e + 1] * swiglu(h, w_gu[e], w_down[e], D_FF_EXPERT).astype(jnp.float32)
    return out.astype(h.dtype)

def setup_inputs(seed: int = 0) -> dict:
    key = jax.random.key(seed)
    ks = iter(jax.random.split(key, 40))
    nrm = lambda shape, scale: jax.random.normal(next(ks), shape, jnp.float32) * scale
    d_in_proj = 2 * D_INNER + 2 * SSD_GROUPS * D_STATE + SSD_HEADS
    dt0 = jnp.exp(jax.random.uniform(next(ks), (N_SSD, SSD_HEADS), jnp.float32,
                                     minval=math.log(1e-3), maxval=math.log(1e-1)))
    inp = {
        "x_prompt": nrm((BATCH, SEQ, D_MODEL), 1.0),
        "x_sample": nrm((DEC_BATCH, DEC_SEQ, D_MODEL), 1.0),
        "state_ssm": nrm((N_SSD, DEC_BATCH, SSD_HEADS, SSD_HEADDIM, D_STATE), 0.1),
        "state_conv": nrm((N_SSD, DEC_BATCH, CONV_W - 1, CONV_DIM), 1.0),
        "norm_mix": 1.0 + nrm((DEPTH, D_MODEL), 0.05),
        "norm_ffn": 1.0 + nrm((DEPTH, D_MODEL), 0.05),
        "norm_final": 1.0 + nrm((D_MODEL,), 0.05),
        "ssd_w_in": nrm((N_SSD, D_MODEL, d_in_proj), D_MODEL ** -0.5),
        "ssd_conv_w": nrm((N_SSD, CONV_W, CONV_DIM), CONV_W ** -0.5),
        "ssd_conv_b": nrm((N_SSD, CONV_DIM), 0.02),
        "ssd_dt_bias": dt0 + jnp.log(-jnp.expm1(-dt0)),
        "ssd_a_log": jnp.log(jax.random.uniform(next(ks), (N_SSD, SSD_HEADS), jnp.float32, minval=1.0, maxval=16.0)),
        "ssd_d": 1.0 + nrm((N_SSD, SSD_HEADS), 0.1),
        "ssd_gnorm": 1.0 + nrm((N_SSD, D_INNER), 0.05),
        "ssd_w_out": nrm((N_SSD, D_INNER, D_MODEL), D_INNER ** -0.5),
        "sgu_w_in": nrm((N_SGU, D_MODEL, 2 * D_SGU), D_MODEL ** -0.5),
        "sgu_b_in": nrm((N_SGU, 2 * D_SGU), 0.02),
        "sgu_ln_g": 1.0 + nrm((N_SGU, D_SGU), 0.05),
        "sgu_ln_b": nrm((N_SGU, D_SGU), 0.02),
        "sgu_w_s": nrm((N_SGU, SGU_HEADS, SGU_CHUNK, SGU_CHUNK), SGU_CHUNK ** -0.5),
        "sgu_b_s": 1.0 + nrm((N_SGU, SGU_HEADS, SGU_CHUNK), 0.1),
        "sgu_w_out": nrm((N_SGU, D_SGU, D_MODEL), D_SGU ** -0.5),
        "ffn_w_gu": nrm((N_SSD, D_MODEL, 2 * D_FF_DENSE), D_MODEL ** -0.5),
        "ffn_w_down": nrm((N_SSD, D_FF_DENSE, D_MODEL), D_FF_DENSE ** -0.5),
        "moe_w_router": nrm((N_SGU, D_MODEL, N_EXPERTS), D_MODEL ** -0.5),
        "moe_w_gu": nrm((N_SGU, N_EXPERTS, D_MODEL, 2 * D_FF_EXPERT), D_MODEL ** -0.5),
        "moe_w_down": nrm((N_SGU, N_EXPERTS, D_FF_EXPERT, D_MODEL), D_FF_EXPERT ** -0.5),
    }
    return inp

def reference(x_prompt, x_sample, state_ssm, state_conv, norm_mix, norm_ffn, norm_final,
              ssd_w_in, ssd_conv_w, ssd_conv_b, ssd_dt_bias, ssd_a_log, ssd_d, ssd_gnorm, ssd_w_out,
              sgu_w_in, sgu_b_in, sgu_ln_g, sgu_ln_b, sgu_w_s, sgu_b_s, sgu_w_out,
              ffn_w_gu, ffn_w_down, moe_w_router, moe_w_gu, moe_w_down):
    hp, hs = x_prompt, x_sample
    ssm_p, conv_p, ssm_s, conv_s, v_s = [], [], [], [], []
    for i in range(DEPTH):
        j = i // 2
        a_p, a_s = rmsnorm(hp, norm_mix[i]), rmsnorm(hs, norm_mix[i])
        if i % 2 == 0:
            prm = (ssd_w_in[j], ssd_conv_w[j], ssd_conv_b[j], ssd_dt_bias[j], ssd_a_log[j],
                   ssd_d[j], ssd_gnorm[j], ssd_w_out[j])
            yp, sp, cp = ssd_mixer(a_p, None, None, *prm)
            ys, ss, cs = ssd_mixer(a_s, state_conv[j], state_ssm[j], *prm)
            ssm_p.append(sp); conv_p.append(cp); ssm_s.append(ss); conv_s.append(cs)
        else:
            prm = (sgu_w_in[j], sgu_b_in[j], sgu_ln_g[j], sgu_ln_b[j], sgu_w_s[j], sgu_b_s[j], sgu_w_out[j])
            yp, _ = sgu_mixer(a_p, *prm)
            ys, vs = sgu_mixer(a_s, *prm)
            v_s.append(vs)
        hp = hp + yp
        hs = hs + ys
        a_p, a_s = rmsnorm(hp, norm_ffn[i]), rmsnorm(hs, norm_ffn[i])
        if i % 2 == 0:
            hp = hp + swiglu(a_p, ffn_w_gu[j], ffn_w_down[j], D_FF_DENSE)
            hs = hs + swiglu(a_s, ffn_w_gu[j], ffn_w_down[j], D_FF_DENSE)
        else:
            hp = hp + moe_swiglu(a_p, moe_w_router[j], moe_w_gu[j], moe_w_down[j])
            hs = hs + moe_swiglu(a_s, moe_w_router[j], moe_w_gu[j], moe_w_down[j])
    y_prompt = rmsnorm(hp, norm_final)
    y_sample = rmsnorm(hs, norm_final)
    return (y_prompt, y_sample, jnp.stack(ssm_p), jnp.stack(conv_p), jnp.stack(ssm_s), jnp.stack(conv_s), jnp.stack(v_s))


_drawn_inputs = setup_inputs


def setup_inputs(seed=0):
    import zlib

    import numpy as np

    out = dict(_drawn_inputs(seed))
    spreads = {}
    factors = {'sgu_ln_b': 2.849}
    for name, (base, spread) in spreads.items():
        noise = np.random.default_rng([zlib.crc32(name.encode()), seed]).standard_normal(out[name].shape)
        drawn = base * np.exp(spread * noise) if base else spread * noise
        out[name] = __import__('jax').numpy.asarray(drawn.astype(out[name].dtype))
    for name, factor in factors.items():
        out[name] = (out[name] * factor).astype(out[name].dtype)
    return out
```

```python
from contextlib import ExitStack

import concourse.bass as bass
from concourse import mybir

F32 = mybir.dt.float32
I32 = mybir.dt.int32
ALU = mybir.AluOpType
ACT = mybir.ActivationFunctionType
AX = mybir.AxisListType.X

P = 128
D = 1024
DT = D // P
NP_ = 256
NS = 8
T = NP_ + NS
ROWS = [P, P, NS]
DI = 2048
IT = DI // P
H = 32
G = 4
CD = 3072
CT = CD // P
FF = 2816
FT = FF // P
E = 8
FE = 3584
ET = FE // P
CAP = 112
CHUNKS = -(-T // CAP)
MORE = E * (CHUNKS - 1)
ITEMS = E + MORE + 1
SLOT = 4096
RING = 7
SSD_RING = 4
SB = 3
EPS = 1e-5
FAR = 10000.0


class Order:

    def __init__(self, eng, sem):
        self.eng, self.sem, self.n, self.base = eng, sem, 0, 0

    def did(self, ins):
        ins.then_inc(self.sem, 1)
        self.n += 1

    def settle(self, but=0):
        self.eng.wait_ge(self.sem, self.base + (self.n - but))


def hybrid_step(nc, i, o):
    ctx = ExitStack()
    with ctx:
        sems = {}

        def S(name):
            if name not in sems:
                sems[name] = ctx.enter_context(nc.semaphore(name))
            return sems[name]

        def sb(name, shape, dt=F32):
            return ctx.enter_context(nc.sbuf_tensor(name, shape, dt))

        ring = sb("ring", [P, RING, SLOT])
        xT = sb("xT", [P, DT, T])
        aT = sb("aT", [P, DT, T])
        sq = sb("sq", [P, 2, T])
        rs = sb("rs", [P, 2, T])
        ident = sb("ident", [P, P])
        ones = sb("ones", [P, P])
        causal = sb("causal", [P, P])
        before = sb("before", [P, P])
        V = sb("V", [P, 240])
        small = sb("small", [P, 64])
        psum = [ctx.enter_context(nc.psum_tensor(f"bank{b}", [P, 512], F32)) for b in range(8)]
        ARENA = 17920
        arena = sb("arena", [P, ARENA])

        class Room:

            def __init__(self, ap, size, at=0):
                self.ap, self.size, self.at = ap, size, at

            def take(self, n):
                self.at += n
                assert self.at <= self.size, (self.at, self.size)
                return self.ap[:, self.at - n:self.at]

        NM = [0, 8]
        NF = [16, 24]
        NFIN, GN, CB_, LG, LB = 32, 40, 56, 80, 96
        CW, BI = 112, 208
        NORM = [NM[0], NF[0], NM[1], NF[1], NFIN]
        dcol = small[:, 0:16]
        w00 = small[:, 16:24]
        b00 = small[:, 24:32]
        dtb = small[0:H, 32:33]
        alog = small[0:H, 33:34]
        aneg = small[0:H, 34:35]

        r = Room(arena, ARENA)
        zT = r.take(IT * T).rearrange("p (t n) -> p t n", t=IT)
        xbc = r.take(CT * T).rearrange("p (t n) -> p t n", t=CT)
        early = r.take(CT * NS * 4 + 2 * 259 + 2 * H * DT // 2 + 256 + 32)
        e_ = Room(early, early.shape[1])
        convS = e_.take(CT * NS * 4).rearrange("p (t b k) -> p t b k", t=CT, b=NS)
        raw = e_.take(2 * 259).rearrange("p (u n) -> p u n", u=2)
        wdt = e_.take(DT * H).rearrange("p (k n) -> p k n", k=DT)
        cs1 = e_.take(256)
        cprod = e_.take(NS * 4).rearrange("p (b k) -> p b k", b=NS)
        l_ = Room(early, early.shape[1])
        fin = l_.take(512)
        hd = l_.take(2 * P).rearrange("p (u n) -> p u n", u=2)
        junk = l_.take(2 * P).rearrange("p (u n) -> p u n", u=2)
        ce = l_.take(512).rearrange("p (u h i) -> p u h i", u=2, h=2)
        el = l_.take(256).rearrange("p (h i) -> p h i", h=2)
        tail = r.take(CT * 11).rearrange("p (t k) -> p t k", t=CT)
        seg = r.take(512).rearrange("p (h c i) -> p h c i", h=2, c=2)
        ex = seg
        mm_ = r.take(1024).rearrange("p (u h c i) -> p u h c i", u=2, h=2, c=2)
        hp = r.take(512)
        xsf = r.take(3 * 512).rearrange("p (k n) -> p k n", k=3)
        dtk = r.take(P)
        dtk_v = dtk.rearrange("p (w c h) -> p w c h", w=2, c=2)
        wend = r.take(96).rearrange("p (k h) -> p k h", k=3)
        sexp = r.take(256).rearrange("p (t w b) -> p t w b", t=IT, w=2)
        dtx = r.take(P).rearrange("p (t b) -> p t b", t=IT)
        ys = r.take(NS)
        dtT = xsf[0:H, 0, 0:T]
        dtw = xsf[0:H, 1, 0:T]
        dtv = xsf[0:H, 2, 0:T]
        LAT = r.take(256)[0:H, :]
        laraw = hp[0:H, 0:256]
        dspr = hp[0:H, 256:512]
        halves = xsf[0:H, 0, 384:512]
        hsel = xsf[0:H, 1, 384:386]
        psel = xsf[0:H, 1, 400:416]
        dle = r.take(64)[0:H, :]
        dsx = r.take(16)[0:H, :]
        ssd_used = r.at
        s = Room(ring[:, SSD_RING:RING, :].rearrange("p r n -> p (r n)"), 3 * SLOT)
        Xdt = s.take(2 * DI).rearrange("p (c n) -> p c n", c=2)
        st = s.take(SB * 1024).rearrange("p (u b n) -> p u b n", u=SB, b=NS)
        bcs = s.take(1024)[0:NS, :]
        sbc = s.take(2 * 1024).rearrange("p (w b n) -> p w b n", w=2, b=NS)
        Btok = s.take(1024).rearrange("p (c n) -> p c n", c=2)
        CBm = s.take(1024).rearrange("p (g c i) -> p g c i", g=G, c=2)
        xtok = ring[:, SSD_RING, 0:3072].rearrange("p (n d) -> p n d", n=3)
        vrow = ring[:, SSD_RING + 1, 0:256].rearrange("p (u d) -> p u d", u=2)
        crow = ring[0:24, SSD_RING + 1, 1024:4096]
        ncv = ring[0:11, SSD_RING + 2, 0:3072]

        hT = arena[:, 0:FT * T].rearrange("p (t n) -> p t n", t=FT)
        fs = arena[:, 16384:16384 + 2 * T].rearrange("p (u n) -> p u n", u=2)
        r = Room(arena, ARENA)
        uT = r.take(IT * T).rearrange("p (t n) -> p t n", t=IT)
        vT = r.take(IT * T).rearrange("p (t n) -> p t n", t=IT)
        vtok = r.take(2 * DI).rearrange("p (c n) -> p c n", c=2)
        wsr = r.take(8 * P).rearrange("p (g j) -> p g j", g=8)
        wsT = r.take(8 * P).rearrange("p (g i) -> p g i", g=8)
        bsr = r.take(P)[0:8, :]
        mus = r.take(T)
        ssm = r.take(2 * NS).rearrange("p (u n) -> p u n", u=2)
        vnew = r.take(DI)[0:NS, :]
        r = Room(arena, ARENA)
        atok = r.take(3 * D).rearrange("p (n d) -> p n d", n=3)
        hE = r.take(ET * CAP).rearrange("p (t c) -> p t c", t=ET)
        xe = r.take(DT * CAP).rearrange("p (t c) -> p t c", t=DT)
        ye = r.take(DT * CAP).rearrange("p (t c) -> p t c", t=DT)
        yt = r.take(D)[0:CAP, :]
        GT = r.take(T)[0:CAP, :]
        Sm = r.take(3 * CAP).rearrange("p (n c) -> p n c", n=3)
        SG = r.take(3 * CAP).rearrange("p (n c) -> p n c", n=3)
        es = r.take(2 * 4 * CAP).rearrange("p (u n) -> p u n", u=2)
        iota = r.take(P)
        wr = r.take(DT * E).rearrange("p (k e) -> p k e", k=DT)
        t38 = [r.take(24).rearrange("p (n e) -> p n e", n=3) for _ in range(8)]
        L, eq, oh1, oh2, L2, gw, msk, pos = t38
        t3 = [r.take(3) for _ in range(8)]
        m1, mx, m2, ed, den, g1, g2, valid = t3
        rev = r.take(E)
        ev = r.take(16)
        cnt = r.take(E)
        pres = r.take(MORE)
        incl = r.take(MORE)
        Q = r.take(3 * (E + MORE)).rearrange("p (n s) -> p n s", n=3)
        gw2 = r.take(3 * MORE).rearrange("p (n s) -> p n s", n=3)
        OJ = r.take((MORE + 1) * MORE).rearrange("p (j s) -> p j s", s=MORE)
        OX = r.take((MORE + 1) * MORE).rearrange("p (j s) -> p j s", s=MORE)
        Aall = r.take(3 * ITEMS).rearrange("p (n j) -> p n j", n=3)
        Gall = r.take(3 * ITEMS).rearrange("p (n j) -> p n j", n=3)
        itf = r.take(ITEMS)
        moe_used = r.at
        iti = sb("iti", [1, ITEMS + 1], I32)
        ioti = sb("ioti", [P, P], I32)
        yrow = arena[:, 12288:12288 + 3072].rearrange("p (n d) -> p n d", n=3)
        assert moe_used <= 12288 and ssd_used <= ARENA, (moe_used, ssd_used)

        w_in = i["ssd_w_in"][0].rearrange("(k p) n -> p k n", p=P)
        dense = []

        def cols(w, kt, c0, width):
            return w.rearrange("(k p) n -> p k n", p=P)[:, :, c0:c0 + width], kt, width

        XO = [16, 17, 18, 19, 20, 21, 22, 23] + list(range(16))
        for c in (8, 9, 4, 5, 6, 7, 0, 1, 2, 3):
            dense.append(cols(i["ssd_w_in"][0], DT, 512 * c, 512))
        for c in range(4):
            dense.append(cols(i["ssd_w_out"][0], IT, 256 * c, 256))
        SSD_TILES = len(dense)
        for c in range(11):
            dense.append((("pair", c), DT, 512))
        for c in range(8):
            dense.append(cols(i["ffn_w_down"][0], FT, 128 * c, 128))
        for c in (4, 5, 6, 7, 0, 1, 2, 3):
            dense.append(cols(i["sgu_w_in"][0], DT, 512 * c, 512))
        for c in range(4):
            dense.append(cols(i["sgu_w_out"][0], IT, 256 * c, 256))
        place, landed, last = [], [0] * RING, [None] * RING
        at = 0
        for n, (src, _, _) in enumerate(dense):
            if n == SSD_TILES:
                at = SSD_RING
            q = at % (SSD_RING if n < SSD_TILES else RING)
            at = q + 1
            landed[q] += 32 if isinstance(src, tuple) else 16
            place.append((q, landed[q], last[q]))
            last[q] = n
        ND = len(dense)
        R0 = at % RING
        eslot = [((R0 + k) % RING, landed[(R0 + k) % RING] + 16 * (k // RING + 1)) for k in range(21)]
        assert all(last[(R0 + k) % RING] == ND - RING + k for k in range(RING))

        def read(n):
            for first, count, name, per, base in ((0, 10, "proj", 4, 0), (10, 4, "o_mm", 2, 0), (14, 11, "ffn", 2, 0),
                                                  (25, 8, "o_mm", 1, DT), (33, 8, "sgu", 4, 0), (41, 4, "o_mm", 2, 2 * DT)):
                if n < first + count:
                    return S(name), base + per * (n - first + 1)

        gu = i["moe_w_gu"][0]
        dn = i["moe_w_down"][0]

        block = ctx.enter_context(nc.Block())
        nk = range(DT)

        def bcast(ap, shape):
            return ap.to_broadcast(shape)

        def col1(k):
            return ident[0:H, k:k + 1].to_broadcast((H, P))

        @block.sync
        def _(sp):
            sp.dma_start(xtok[:, 0:2, :], i["x_prompt"][0].rearrange("(n p) d -> p n d", p=P)).then_inc(S("x_in"), 16)
            sp.dma_start(xtok[0:NS, 2, :], i["x_sample"].rearrange("b s d -> (b s) d")).then_inc(S("x_in"), 16)
            sp.dma_start(wdt, w_in[:, :, DI + CD:DI + CD + H]).then_inc(S("wdt_in"), 16)
            for n, (src, kt, width) in enumerate(dense):
                q, _, prev = place[n]
                if prev is not None:
                    sp.wait_ge(*read(prev))
                elif n >= SSD_TILES:
                    sp.wait_ge(S("ssd_over"), 1)
                    for k in range(SB):
                        sp.wait_ge(S(f"so{k}"), 16 * len(range(k, IT, SB)))
                    sp.wait_ge(S("conv_out"), 48)
                dst = ring[:, q, 0:kt * width].rearrange("p (k n) -> p k n", k=kt)
                if isinstance(src, tuple):
                    src = i["ffn_w_gu"][0].rearrange("(k p) (u n) -> p k u n", p=P, u=2)[
                        :, :, :, 256 * src[1]:256 * src[1] + 256]
                    for u in range(2):
                        sp.dma_start(dst[:, :, 256 * u:256 * u + 256], src[:, :, u, :]).then_inc(S(f"w{q}"), 16)
                else:
                    sp.dma_start(dst, src).then_inc(S(f"w{q}"), 16)

            def expert(e, item):
                for s_ in range(21):
                    q, _ = eslot[s_]
                    if item is None and s_ < RING:
                        sp.wait_ge(*read(ND - RING + s_))
                    else:
                        sp.wait_ge(S("w_used"), s_ - RING + 1 if item is None else item * 21 + (s_ - RING + 1))
                    if s_ < 14:
                        c0 = 512 * (s_ // 2) + FE * (s_ % 2)
                        src = gu[bass.ds(e, 1), :, c0:c0 + 512].rearrange("e (k p) n -> p (e k) n", p=P)
                    else:
                        src = dn[bass.ds(e, 1), 512 * (s_ - 14):512 * (s_ - 13), :].rearrange(
                            "e (k p) n -> p (e k) n", p=P)
                    dst = ring[:, q, :].rearrange("p (k n) -> p k n", k=8 if s_ < 14 else 4)
                    sp.dma_start(dst, src).then_inc(S(f"w{q}"), 16)

            expert(0, None)
            with sp.Fori(1, E) as e:
                expert(e, e)
            sp.wait_ge(S("items_ready"), 1)
            n_items = sp.value_load(iti[0:1, ITEMS:ITEMS + 1], min_val=E, max_val=E + MORE)
            with sp.If(n_items > E):
                with sp.Fori(E, n_items) as item:
                    e = sp.value_load(iti[0:1, bass.ds(item, 1)], min_val=0, max_val=E - 1)
                    expert(e, item)
            sp.wait_ge(S("y_stored"), 1)
            sp.dma_start(o[0][0].rearrange("(n p) d -> p n d", p=P), yrow[:, 0:2, :]).then_inc(S("y_out"), 16)
            sp.dma_start(o[1].rearrange("b s d -> (b s) d"), yrow[0:NS, 2, :]).then_inc(S("y_out"), 16)
            sp.wait_ge(S("y_out"), 32)

        @block.gpsimd
        def _(pool):
            own = Order(pool, S("pool_own"))
            own.did(pool.memset(ident[:, :], 0.0))
            own.did(pool.memset(ones[:, :], 1.0))
            own.did(pool.memset(causal[:, :], 1.0))
            own.did(pool.memset(before[:, :], 1.0))
            own.settle()
            pool.affine_select(out=ident[:, :], in_=ident[:, :], compare_op=ALU.not_equal, fill=1.0, base=0,
                               pattern=[[-1, P]], channel_multiplier=1).then_inc(S("consts"), 1)
            pool.affine_select(out=causal[:, :], in_=causal[:, :], compare_op=ALU.is_ge, fill=0.0, base=0,
                               pattern=[[1, P]], channel_multiplier=-1).then_inc(S("consts"), 1)
            pool.affine_select(out=before[:, :], in_=before[:, :], compare_op=ALU.is_gt, fill=0.0, base=0,
                               pattern=[[1, P]], channel_multiplier=-1).then_inc(S("consts"), 1)
            pool.iota(ioti[:, :], pattern=[[1, P]], base=0, channel_multiplier=0).then_inc(S("iota"), 1)
            sd = i["ssd_d"].rearrange("o (t w) -> o w t", w=2)
            for w in range(2):
                pool.dma_start(dcol[64 * w:64 * w + 64, :], sd[:, w, :].to_broadcast((64, IT)), allow_slow_non_contiguous=True).then_inc(S("cols_in"), 16)
            pool.dma_start(w00, i["sgu_w_s"][:, :, 0, 0].to_broadcast((P, 8)), allow_slow_non_contiguous=True).then_inc(S("cols_in"), 16)
            pool.dma_start(b00, i["sgu_b_s"][:, :, 0].to_broadcast((P, 8)), allow_slow_non_contiguous=True).then_inc(S("cols_in"), 16)
            pool.dma_start(o[5][0, :, 0:2, :], i["state_conv"][0, :, 1:3, :]).then_inc(S("conv_out"), 16)

            h_in = i["state_ssm"][0].rearrange("b (t w) q n -> t (w q) b n", w=2)
            h_out = o[4][0].rearrange("b (t w) q n -> t (w q) b n", w=2)

            def state_in(t):
                pool.dma_start(st[:, t % SB], h_in[t]).then_inc(S(f"st{t % SB}"), 16)

            def weighted(g):
                pool.wait_ge(S("wend_ready"), 1)
                pool.wait_ge(S("xdt_ready"), 4 * g + 4)
                if g:
                    pool.wait_ge(S("misc"), 4 + 6 * (g - 1) + 2)
                for k, c in ((0, 0), (1, 0), (2, 1)):
                    pool.tensor_tensor(
                        xsf[:, k, :].rearrange("p (h q) -> p h q", q=64),
                        Xdt[:, c, 512 * g:512 * g + 512].rearrange("p (h q) -> p h q", q=64),
                        wend[:, k, 8 * g:8 * g + 8].unsqueeze(2).to_broadcast((P, 8, 64)),
                        ALU.mult).then_inc(S("weighted"), 1)

            pool.wait_ge(S("start_over"), 1)
            for t in range(SB - 1):
                state_in(t)
            weighted(0)
            for t in range(IT):
                if t % 4 == 0 and t // 4 + 1 < G:
                    weighted(t // 4 + 1)
                pool.wait_ge(S("y_sample"), t + 1)
                pool.dma_start(h_out[t], st[:, t % SB]).then_inc(S(f"so{t % SB}"), 16)
                if t + SB - 1 < IT:
                    if t >= 1:
                        pool.wait_ge(S(f"so{(t - 1) % SB}"), 16 * ((t - 1) // SB + 1))
                    state_in(t + SB - 1)
            pool.wait_ge(S("ncv_ready"), 1)
            pool.dma_start(o[3][0, 0], ncv[0:3, :]).then_inc(S("conv_out"), 16)
            pool.dma_start(o[5][0, :, 2, :], ncv[3:11, :]).then_inc(S("conv_out"), 16)
            for k in range(SB):
                pool.wait_ge(S(f"so{k}"), 16 * len(range(k, IT, SB)))
            pool.wait_ge(S("conv_out"), 48)
            pool.wait_ge(S("fin_out"), 16 * G)
            pool.wait_ge(S("v_out"), 16)

        @block.scalar
        def _(act):
            own = Order(act, S("act_own"))
            rows = [("norm_mix", 0, 0), ("norm_mix", 1, 8), ("norm_ffn", 0, 16), ("norm_ffn", 1, 24)]
            for name, row, at_ in rows:
                act.dma_start(vrow[at_:at_ + 8, 0, :], i[name][row].rearrange("(t p) -> t p", p=P)).then_inc(S("v_in"), 16)
            for src, at_, n in ((i["norm_final"], 32, 8), (i["ssd_gnorm"][0], 40, 16), (i["ssd_conv_b"][0], 56, 24),
                                (i["sgu_ln_g"][0], 80, 16), (i["sgu_ln_b"][0], 96, 16)):
                act.dma_start(vrow[at_:at_ + n, 0, :], src.rearrange("(t p) -> t p", p=P)).then_inc(S("v_in"), 16)
            act.dma_start(vrow[0:96, 1, :], i["ssd_conv_w"][0].rearrange("k (t p) -> (k t) p", p=P)).then_inc(S("v_in"), 16)
            act.dma_start(vrow[96:128, 1, :], i["sgu_b_in"][0].rearrange("(t p) -> t p", p=P)).then_inc(S("v_in"), 16)
            act.dma_start(crow, i["state_conv"][0].rearrange("b k n -> (b k) n")).then_inc(S("crow_in"), 16)
            act.dma_start(dtb, i["ssd_dt_bias"].rearrange("o h -> h o"), allow_slow_non_contiguous=True).then_inc(S("dtw_in"), 16)
            act.dma_start(alog, i["ssd_a_log"].rearrange("o h -> h o"), allow_slow_non_contiguous=True).then_inc(S("dtw_in"), 16)
            act.wait_ge(S("vec_tr"), 1)
            act.activation(V[:, :], psum[5][:, 0:240], ACT.Copy).then_inc(S("vec_ready"), 1)

            def norm(n, before_):
                for m in range(DT):
                    act.wait_ge(S("x_ready"), DT * n + m + 1)
                    if m >= 2 or n > 0:
                        act.wait_ge(S("sq_used"), DT * n + before_ + m - 1)
                    act.activation(sq[:, m % 2, :], xT[:, m, :], ACT.Square).then_inc(S("sq_ready"), 1)
                act.wait_ge(S("ms_ready"), n + 1)
                act.activation(rs[:, 1, :], rs[:, 0, :], ACT.Sqrt).then_inc(S("root_ready"), 1)

            norm(0, 0)
            act.wait_ge(S("dtw_in"), 32)
            act.activation(aneg, alog, ACT.Exp).then_inc(S("a_exp"), 1)
            for n in range(CT):
                act.wait_ge(S("proj"), n + 1)
                if n >= 2:
                    act.wait_ge(S("conv_done"), n - 1)
                if n == 0:
                    act.wait_ge(S("pads"), 2)
                    act.wait_ge(S("convS_ready"), 2)
                act.activation(raw[:, n % 2, 3:259], psum[n % 2][:, 0:NP_], ACT.Copy).then_inc(S("raw_ready"), 1)
                act.activation(convS[:, XO[n], :, 3], psum[n % 2][:, NP_:T], ACT.Copy).then_inc(S("raw_ready"), 1)
                if n == 4:
                    act.wait_ge(S("dt_abs"), 1)
                    own.did(act.activation(dtw, dtw, ACT.Exp, scale=-1.0))
                    own.settle()
                    act.activation(dtw, dtw, ACT.Ln, bias=1.0).then_inc(S("dt_log"), 1)
                if n == 8:
                    act.wait_ge(S("dsx_dt"), 1)
                    act.activation(dsx[:, 8:16], dsx[:, 8:16], ACT.Exp).then_inc(S("dsx_ready"), 1)
                    act.wait_ge(S("wend_in"), 1)
                    act.activation(wend, wend, ACT.Exp).then_inc(S("wend_ready"), 1)
                if n >= 1:
                    act.wait_ge(S("conv_done"), n)
                    t = XO[n - 1]
                    act.activation(xbc[:, t, :], xbc[:, t, :], ACT.Silu, bias=V[:, CB_ + t:CB_ + t + 1]).then_inc(S("xbc_ready"), 1)
                if n == 10:
                    for c in range(2):
                        act.wait_ge(S("misc"), c + 1)
                        act.activation(Btok[:, c, :], psum[5 + c][:, :], ACT.Copy).then_inc(S("misc_free"), 1)
                if n == 11:
                    for c in range(2):
                        act.wait_ge(S("misc"), c + 3)
                        act.activation(bcs[:, 512 * c:512 * c + 512], psum[5 + c][0:NS, :], ACT.Copy).then_inc(S("misc_free"), 1)
            act.wait_ge(S("conv_done"), CT)
            act.activation(xbc[:, 15, :], xbc[:, 15, :], ACT.Silu, bias=V[:, CB_ + 15:CB_ + 16]).then_inc(S("xbc_ready"), 1)

            fin_out = o[2][0, 0].rearrange("(g t w) q n -> g (w q) t n", g=G, w=2)
            misc = 4
            for t in range(IT + 1):
                if t < IT:
                    act.wait_ge(S("proj"), CT + t + 1)
                    act.activation(zT[:, t, :], psum[(CT + t) % 2][:, 0:T], ACT.Copy).then_inc(S("z_ready"), 1)
                    if t % 4 == 0:
                        g = t // 4
                        act.wait_ge(S("misc"), misc + 1)
                        act.activation(hp, psum[5 + misc % 2][:, :], ACT.Copy).then_inc(S("misc_free"), 1)
                        misc += 1
                        act.wait_ge(S("misc"), misc + 1)
                        if g:
                            act.wait_ge(S("fin_out"), 16 * g)
                        act.activation(fin, psum[5 + misc % 2][:, :], ACT.Copy).then_inc(S("misc_free"), 1)
                        misc += 1
                        act.wait_ge(S("misc_free"), misc)
                        act.dma_start(fin_out[g], fin.rearrange("p (t n) -> p t n", t=4)).then_inc(S("fin_out"), 16)
                        if g:
                            act.wait_ge(S("y_sample"), t)
                        for w in range(2):
                            for half in range(2):
                                act.wait_ge(S("misc"), misc + 1)
                                act.activation(sbc[:, w, 4 * half:4 * half + 4, :],
                                               psum[5 + misc % 2][:, :].rearrange("p (b n) -> p b n", b=4),
                                               ACT.Copy).then_inc(S("misc_free"), 1)
                                misc += 1
                    act.wait_ge(S("seg_ready"), t + 1)
                    if t:
                        act.wait_ge(S("ce_ready"), t)
                    act.activation(el, psum[2 + t % 2][:, :].rearrange("p (h c i) -> p h c i", h=2, c=2)[:, :, 1, :],
                                   ACT.Exp).then_inc(S("el_ready"), 1)
                    if t:
                        act.wait_ge(S("m_ready"), t)
                    act.activation(ex, seg, ACT.Exp).then_inc(S("ex_ready"), 1)
                    act.wait_ge(S(f"st{t % SB}"), 16 * (t // SB + 1))
                    act.wait_ge(S("sexp_ready"), 2)
                    for b in range(NS):
                        n = NS * t + b
                        if n >= 2:
                            act.wait_ge(S("upd"), n - 1)
                        act.activation(hd[:, n % 2, :], st[:, t % SB, b, :], ACT.Copy,
                                       scale=sexp[:, t, 1, b:b + 1]).then_inc(S("decayed"), 1)
            act.wait_ge(S("z_ready"), IT)
            for g in range(G):
                act.activation(zT[:, 4 * g:4 * g + 4, :], zT[:, 4 * g:4 * g + 4, :], ACT.Silu).then_inc(S("gate_ready"), 1)
            for g in range(G):
                for k in range(4):
                    n = 4 * g + k
                    act.wait_ge(S("gated"), n + 1)
                    act.wait_ge(S("sq_used"), DT + n - 1)
                    act.activation(sq[:, n % 2, :], zT[:, n, :], ACT.Square).then_inc(S("sq_ready"), 1)
                act.wait_ge(S("gms_ready"), g + 1)
                act.activation(rs[:, 1, :], rs[:, 0, :], ACT.Sqrt).then_inc(S("groot_ready"), 1)
            norm(1, IT)
            act.dma_start(wsr, i["sgu_w_s"][0].rearrange("g i j -> i g j")).then_inc(S("ws_in"), 16)
            act.dma_start(bsr, i["sgu_b_s"][0]).then_inc(S("bs_in"), 16)
            for n in range(FT):
                act.wait_ge(S("ffn"), n + 1)
                if n >= 2:
                    act.wait_ge(S("ffn_h"), n - 1)
                act.activation(fs[:, n % 2, :], psum[2 * (n % 2)][:, 0:T], ACT.Silu).then_inc(S("ffn_silu"), 1)
            norm(2, IT)
            for n in range(2 * IT):
                t = n % IT
                act.wait_ge(S("sgu"), n + 1)
                dst = (vT if n < IT else uT)[:, t, :]
                c = BI + (IT + t if n < IT else t)
                act.activation(dst, psum[n % 2][:, 0:T], ACT.Gelu, bias=V[:, c:c + 1]).then_inc(S("gelu"), 1)
                if n >= IT:
                    act.wait_ge(S("v_centred"), t + 1)
                    act.wait_ge(S("sq_used"), 3 * DT + IT + t - 1)
                    act.activation(sq[:, t % 2, :], vT[:, t, :], ACT.Square).then_inc(S("sq_ready"), 1)
            act.wait_ge(S("vms_ready"), 1)
            act.activation(rs[:, 1, :], rs[:, 0, :], ACT.Sqrt).then_inc(S("vroot_ready"), 1)
            act.wait_ge(S("vnew_ready"), 4)
            act.dma_start(o[6].rearrange("o b s d -> (o b s) d"), vnew).then_inc(S("v_out"), 16)
            act.wait_ge(S("sp_done"), IT)
            act.dma_start(wr, i["moe_w_router"][0].rearrange("(k p) e -> p k e", p=P)).then_inc(S("wr_in"), 16)
            norm(3, 2 * IT)
            act.wait_ge(S("diff_ready"), 1)
            act.activation(ed, ed, ACT.Exp).then_inc(S("ediff_ready"), 1)
            act.wait_ge(S("items_ready"), 1)
            n_items = act.value_load(iti[0:1, ITEMS:ITEMS + 1], min_val=E, max_val=E + MORE)
            with act.Fori(0, n_items) as item:
                for j in range(7):
                    act.wait_ge(S("w_used"), item * 21 + (2 * j + 2))
                    if j >= 2:
                        act.wait_ge(S("e_h"), item * 7 + (j - 1))
                    act.activation(es[:, j % 2, :], psum[2 * (j % 2)][:, 0:4 * CAP], ACT.Silu).then_inc(S("e_silu"), 1)
                act.wait_ge(S("w_used"), item * 21 + 21)
                for half in range(2):
                    act.activation(ye[:, 4 * half:4 * half + 4, :],
                                   psum[4 + half][:, 0:4 * CAP].rearrange("p (m c) -> p m c", m=4),
                                   ACT.Copy).then_inc(S("e_y"), 1)
            norm(4, 2 * IT)

        @block.tensor
        def _(pe):
            mm, tr = pe.matmul, pe.transpose
            pe.wait_ge(S("consts"), 3)
            pe.wait_ge(S("v_in"), 16 * 11)
            tr(psum[5][:, 0:112], vrow[0:112, 0, :], ident[0:112, 0:112])
            tr(psum[5][:, 112:240], vrow[:, 1, :], ident[:, :]).then_inc(S("vec_tr"), 1)
            pe.wait_ge(S("x_in"), 32)
            for m in nk:
                if m >= 2:
                    pe.wait_ge(S("x_ready"), m - 1)
                for n in range(3):
                    ins = tr(psum[m % 2][:, P * n:P * n + ROWS[n]], xtok[0:ROWS[n], n, P * m:P * m + P],
                             ident[0:ROWS[n], 0:ROWS[n]])
                ins.then_inc(S("x_tr"), 1)
            pe.wait_ge(S("crow_in"), 16)
            pe.wait_ge(S("vec_ready"), 1)
            for half in range(2):
                for t in range(12):
                    ins = tr(psum[5 + half][:, 24 * t:24 * t + 24], crow[:, P * (12 * half + t):P * (12 * half + t) + P],
                             ident[0:24, 0:24])
                ins.then_inc(S("crow_tr"), 1)

            def norm(n, before_):
                for m in nk:
                    pe.wait_ge(S("sq_ready"), DT * n + before_ + m + 1)
                    mm(psum[7][:, 0:T], ones[:, :], sq[:, m % 2, :], start=(m == 0), stop=(m == DT - 1)).then_inc(S("sq_used"), 1)

            def weight(n):
                q, landed_, _ = place[n]
                _, kt, width = dense[n]
                pe.wait_ge(S(f"w{q}"), landed_)
                return ring[:, q, 0:kt * width].rearrange("p (k n) -> p k n", k=kt)

            norm(0, 0)
            pe.wait_ge(S("wdt_in"), 16)
            pe.wait_ge(S("convS_ready"), 2)
            for k in nk:
                pe.wait_ge(S("a_ready"), k + 1)
                ins = mm(psum[6][0:H, 0:T], wdt[:, k, :], aT[:, k, :], start=(k == 0), stop=(k == DT - 1))
            ins.then_inc(S("dt_mm"), 1)

            def xtr(q):
                pe.wait_ge(S("xbc_ready"), 8 + q + 1)
                if q >= 2:
                    pe.wait_ge(S("xdt_ready"), q - 1)
                for c in range(2):
                    ins = tr(psum[2 + q % 2][:, P * c:P * c + P], xbc[:, q, P * c:P * c + P], ident[:, :])
                ins.then_inc(S("xtr"), 1)

            for n in range(CT):
                if n % 4 == 0:
                    w = weight(n // 4)
                if n >= 2:
                    pe.wait_ge(S("raw_ready"), 2 * (n - 1))
                for k in nk:
                    ins = mm(psum[n % 2][:, 0:T], w[:, k, P * (n % 4):P * (n % 4) + P], aT[:, k, :],
                             start=(k == 0), stop=(k == DT - 1))
                ins.then_inc(S("proj"), 1)
                if n == 7:
                    pe.wait_ge(S("dt_ready"), 1)
                    for c in range(2):
                        tr(psum[6][:, H * c:H * c + H], dtT[:, P * c:P * c + P], ident[0:H, 0:H])
                    for c in range(2):
                        tr(psum[6][:, 64 + H * c:64 + H * c + H], LAT[:, P * c:P * c + P], ident[0:H, 0:H])
                    mm(psum[6][:, P:P + 64], ones[0:H, :], dle, start=True, stop=True).then_inc(S("dtk_tr"), 1)
                if n == 9:
                    pe.wait_ge(S("spread_ready"), 1)
                    mm(psum[6][:, 256:512], halves, dspr, start=True, stop=True).then_inc(S("sexp_mm"), 1)
                if n == 10:
                    pe.wait_ge(S("xbc_ready"), 8)
                    pe.wait_ge(S("sexp_ready"), 2)
                    for c in range(2):
                        for g in range(G):
                            ins = tr(psum[5 + c][:, P * g:P * g + P], xbc[:, 16 + g, P * c:P * c + P], ident[:, :])
                        ins.then_inc(S("misc"), 1)
                    for half in range(2):
                        for g in (2 * half, 2 * half + 1):
                            for c in range(2):
                                a = 256 * (g % 2) + P * c
                                ins = mm(psum[2 + half][:, a:a + P], xbc[:, 16 + g, P * c:P * c + P],
                                         xbc[:, 20 + g, P * c:P * c + P], start=True, stop=True)
                        ins.then_inc(S("cb"), 1)
                if n == 11:
                    for w_ in range(2):
                        pe.wait_ge(S("misc_free"), w_ + 1)
                        for g in range(G):
                            ins = tr(psum[5 + w_][0:NS, P * g:P * g + P], xbc[:, 16 + 4 * w_ + g, NP_:T], ident[:, :])
                        ins.then_inc(S("misc"), 1)
                    pe.wait_ge(S("cbm_ready"), 2)
                if n >= 12:
                    xtr(n - 12)
            for q in range(12, IT):
                xtr(q)

            misc = 4
            for t in range(IT + 1):
                if t < IT:
                    n = CT + t
                    if t % 4 == 0:
                        w = weight(n // 4)
                    if t >= 2:
                        pe.wait_ge(S("z_ready"), t - 1)
                    if t == 0:
                        pe.wait_ge(S("raw_ready"), 2 * CT)
                    for k in nk:
                        ins = mm(psum[n % 2][:, 0:T], w[:, k, P * (t % 4):P * (t % 4) + P], aT[:, k, :],
                                 start=(k == 0), stop=(k == DT - 1))
                    ins.then_inc(S("proj"), 1)
                if t:
                    u = t - 1
                    pe.wait_ge(S("m_ready"), u + 1)
                    pe.wait_ge(S("ce_ready"), u + 1)
                    if u >= 1:
                        pe.wait_ge(S("y_done"), u)
                    if u % 4 == 0:
                        pe.wait_ge(S("misc_free"), 4 + 6 * (u // 4) + 1)
                    for h in range(2):
                        out = psum[4][64 * h:64 * h + 64, :]
                        xd = slice(P * u + 64 * h, P * u + 64 * h + 64)
                        mm(out[:, 0:P], Xdt[:, 0, xd], mm_[:, u % 2, h, 0, :], start=True, stop=True)
                        mm(out[:, P:2 * P], Xdt[:, 1, xd], mm_[:, u % 2, h, 1, :], start=True, stop=False)
                        hx = P * (u % 4) + 64 * h
                        ins = mm(out[:, P:2 * P], hp[:, hx:hx + 64], ce[:, u % 2, h, :], start=False, stop=True)
                    ins.then_inc(S("y_mm"), 1)
                if t < IT:
                    if t % 4 == 0:
                        g = t // 4
                        gs = slice(P * g, P * g + P)
                        pe.wait_ge(S("weighted"), 3 * g + 3)
                        pe.wait_ge(S("misc_free"), misc - 1)
                        mm(psum[5 + misc % 2][:, :], Btok[:, 0, gs], xsf[:, 0, :], start=True, stop=True).then_inc(S("misc"), 1)
                        misc += 1
                        pe.wait_ge(S("misc_free"), misc - 1)
                        for q in range(4):
                            for c in range(2):
                                ins = mm(psum[5 + misc % 2][:, P * q:P * q + P], xsf[:, 1 + c, P * q:P * q + P],
                                         Btok[:, c, gs], start=(c == 0), stop=(c == 1))
                        ins.then_inc(S("misc"), 1)
                        misc += 1
                        for w_ in range(2):
                            for half in range(2):
                                pe.wait_ge(S("misc_free"), misc - 1)
                                for b in range(4):
                                    ins = mm(psum[5 + misc % 2][:, P * b:P * b + P],
                                             ident[0:NS, 4 * half + b:4 * half + b + 1].to_broadcast((NS, P)),
                                             bcs[:, 512 * w_ + P * g:512 * w_ + P * g + P], start=True, stop=True)
                                ins.then_inc(S("misc"), 1)
                                misc += 1
                    if t >= 2:
                        pe.wait_ge(S("seg_ready"), t - 1)
                        pe.wait_ge(S("el_ready"), t - 1)
                    if t == 0:
                        pe.wait_ge(S("xdt_ready"), IT)
                    for h in range(2):
                        ins = mm(psum[2 + t % 2][:, 256 * h:256 * h + 256], col1(2 * t + h), LAT, start=True, stop=True)
                    ins.then_inc(S("la"), 1)
            pe.wait_ge(S("tail_ready"), 1)
            for q in range(6):
                pe.wait_ge(S("misc_free"), misc - (1 if q else 0))
                for k in range(4):
                    ins = tr(psum[5 + misc % 2][0:11, P * k:P * k + P], tail[:, 4 * q + k, :], ident[:, :])
                ins.then_inc(S("misc"), 1)
                misc += 1
            for g in range(G):
                if g:
                    pe.wait_ge(S("gms_ready"), g)
                for k in range(4):
                    pe.wait_ge(S("sq_ready"), DT + 4 * g + k + 1)
                    mm(psum[7][:, 0:T], ones[:, :], sq[:, k % 2, :], start=(k == 0), stop=(k == 3)).then_inc(S("sq_used"), 1)

            def out_proj(n0, tiles, kt, width, src, ready, ready_of, xbase):
                m = 0
                for n in range(n0, n0 + tiles):
                    w = weight(n)
                    for c in range(width // P):
                        if m >= 2:
                            pe.wait_ge(S("x_ready"), xbase + m - 1)
                        for k in range(kt):
                            if m == 0:
                                pe.wait_ge(S(ready), ready_of + k + 1)
                            ins = mm(psum[m % 2][:, 0:T], w[:, k, P * c:P * c + P], src[:, k, :],
                                     start=(k == 0), stop=(k == kt - 1))
                        ins.then_inc(S("o_mm"), 1)
                        m += 1

            pe.wait_ge(S("z_ready"), IT)
            out_proj(10, 4, IT, 256, zT, "yg_ready", 0, DT)
            norm(1, IT)
            n0 = SSD_TILES
            for p in range(FT):
                if p % 2 == 0:
                    w = weight(n0 + p // 2)
                if p >= 2:
                    pe.wait_ge(S("ffn_h"), p - 1)
                for u in range(2):
                    for k in nk:
                        if p == 0 and u == 0:
                            pe.wait_ge(S("a_ready"), DT + k + 1)
                        c = 256 * u + P * (p % 2)
                        ins = mm(psum[2 * (p % 2) + u][:, 0:T], w[:, k, c:c + P], aT[:, k, :],
                                 start=(k == 0), stop=(k == DT - 1))
                ins.then_inc(S("ffn"), 1)
            pe.wait_ge(S("ffn_h"), FT)
            out_proj(n0 + 11, 8, FT, 128, hT, "ffn_h", 0, 2 * DT)
            norm(2, IT)
            n0 += 19
            pe.wait_ge(S("ws_in"), 16)
            for half in range(2):
                for g in range(4):
                    ins = tr(psum[4 + half][:, P * g:P * g + P], wsr[:, 4 * half + g, :], ident[:, :])
                ins.then_inc(S("ws_tr"), 1)

            def vtr(t):
                pe.wait_ge(S("vn_ready"), t + 1)
                if t >= 2:
                    pe.wait_ge(S("vtok_ready"), t - 1)
                for c in range(2):
                    ins = tr(psum[4 + t % 2][:, P * c:P * c + P], vT[:, t, P * c:P * c + P], ident[:, :])
                ins.then_inc(S("vtr"), 1)

            for n in range(2 * IT):
                if n % 4 == 0:
                    w = weight(n0 + n // 4)
                if n >= 2:
                    pe.wait_ge(S("gelu"), n - 1)
                for k in nk:
                    if n == 0:
                        pe.wait_ge(S("a_ready"), 2 * DT + k + 1)
                    ins = mm(psum[n % 2][:, 0:T], w[:, k, P * (n % 4):P * (n % 4) + P], aT[:, k, :],
                             start=(k == 0), stop=(k == DT - 1))
                ins.then_inc(S("sgu"), 1)
                if 1 <= n <= IT:
                    pe.wait_ge(S("gelu"), n)
                    ins = mm(psum[7][:, 0:T], ones[:, :], vT[:, n - 1, :], start=(n == 1), stop=(n == IT))
                    if n == IT:
                        ins.then_inc(S("v_sum"), 1)
                if n >= IT + 1:
                    t = n - IT - 1
                    pe.wait_ge(S("sq_ready"), 3 * DT + IT + t + 1)
                    mm(psum[6][:, 0:T], ones[:, :], sq[:, t % 2, :], start=(t == 0), stop=False).then_inc(S("sq_used"), 1)
            pe.wait_ge(S("sq_ready"), 3 * DT + 2 * IT)
            mm(psum[6][:, 0:T], ones[:, :], sq[:, 1, :], start=False, stop=True).then_inc(S("sq_used"), 1)
            pe.wait_ge(S("wsT_ready"), 2)
            for t in range(IT):
                vtr(t)
            pe.wait_ge(S("vtok_ready"), IT)
            pe.wait_ge(S("bs_in"), 16)
            pe.wait_ge(S("gelu"), 2 * IT)
            for t in range(IT):
                g = t // 2
                if t >= 2:
                    pe.wait_ge(S("sp_done"), t - 1)
                for c in range(2):
                    out = psum[2 + t % 2][:, P * c:P * c + P]
                    mm(out, vtok[:, c, P * t:P * t + P], wsT[:, g, :], start=True, stop=False)
                    ins = mm(out, ident[0:8, g:g + 1].to_broadcast((8, P)), bsr, start=False, stop=True)
                ins.then_inc(S("sp_mm"), 1)
            for q in range(4):
                if q:
                    pe.wait_ge(S("vnew_ready"), q)
                for k in range(4):
                    ins = tr(psum[6][0:NS, P * k:P * k + P], vT[:, 4 * q + k, NP_:T], ident[:, :])
                ins.then_inc(S("vnew_tr"), 1)
            out_proj(n0 + 8, 4, IT, 256, uT, "sp_done", 0, 3 * DT)
            norm(3, 2 * IT)
            pe.wait_ge(S("wr_in"), 16)
            for n in range(3):
                for k in nk:
                    if n == 0:
                        pe.wait_ge(S("a_ready"), 3 * DT + k + 1)
                    ins = mm(psum[4][0:ROWS[n], 8 * n:8 * n + 8], aT[:, k, P * n:P * n + ROWS[n]], wr[:, k, :],
                             start=(k == 0), stop=(k == DT - 1))
            ins.then_inc(S("logits"), 1)
            for n in range(3):
                for half in range(2):
                    u = 2 * n + half
                    if u >= 2:
                        pe.wait_ge(S("atok_ready"), u - 1)
                    for k in range(4):
                        m = 4 * half + k
                        ins = tr(psum[half][0:ROWS[n], P * k:P * k + P], aT[:, m, P * n:P * n + ROWS[n]], ident[:, :])
                    ins.then_inc(S("atok_tr"), 1)
            pe.wait_ge(S("mask_ready"), 1)
            for n in range(4):
                for q in range(min(n + 1, 3)):
                    ins = mm(psum[5][:, 8 * n:8 * n + 8], (before if q == n else ones)[:, :], msk[:, q, :],
                             start=(q == 0), stop=(q == min(n, 2)))
            ins.then_inc(S("ranks"), 1)

            def gather(free, item_ready):
                item_ready()
                for half in range(2):
                    free(half)
                    for k in range(4):
                        m = 4 * half + k
                        for n in range(3):
                            ins = mm(psum[7 - half][:, CAP * k:CAP * k + CAP], atok[0:ROWS[n], n, P * m:P * m + P],
                                     Sm[0:ROWS[n], n, :], start=(n == 0), stop=(n == 2))
                    ins.then_inc(S("m_mm"), 1)

            def spread(base, first):
                pe.wait_ge(S("m_free"), base)
                first()
                for n in range(3):
                    ins = tr(psum[6][0:CAP, P * n:P * n + ROWS[n]], SG[0:ROWS[n], n, :], ident[0:ROWS[n], 0:ROWS[n]])
                ins.then_inc(S("m_mm"), 1)
                for half in range(2):
                    if half:
                        pe.wait_ge(S("m_free"), base + 1)
                    for k in range(4):
                        ins = tr(psum[7 - half][0:CAP, P * k:P * k + P], ye[:, 4 * half + k, :], ident[:, :])
                    ins.then_inc(S("m_mm"), 1)
                pe.wait_ge(S("m_free"), base + 3)
                for m in nk:
                    if m:
                        pe.wait_ge(S("m_free"), base + 3 + m - 1)
                    mm(psum[7 - m % 2][:, 0:T], yt[:, P * m:P * m + P], GT, start=True, stop=True).then_inc(S("m_mm"), 1)

            pe.wait_ge(S("atok_ready"), 6)
            gather(lambda half: None, lambda: pe.wait_ge(S("s_ready"), 1))
            n_items = pe.value_load(iti[0:1, ITEMS:ITEMS + 1], min_val=E, max_val=E + MORE)
            pe.wait_ge(S("xe_ready"), 2)
            with pe.Fori(0, n_items) as item:
                def slot(s_):
                    q, landed = eslot[s_]
                    pe.wait_ge(S(f"w{q}"), item * (3 * 16) + landed)
                    return ring[:, q, :]

                pe.wait_ge(S("xe_ready"), item * 2 + 2)
                for j in range(7):
                    if j >= 2:
                        pe.wait_ge(S("e_h"), item * 7 + (j - 1))
                    for u in range(2):
                        w = slot(2 * j + u).rearrange("p (k n) -> p k n", k=8)
                        for m in range(4):
                            for k in nk:
                                ins = mm(psum[2 * (j % 2) + u][:, CAP * m:CAP * m + CAP], w[:, k, P * m:P * m + P],
                                         xe[:, k, :], start=(k == 0), stop=(k == DT - 1))
                        ins.then_inc(S("w_used"), 1)
                    if j == 1:
                        spread(item * 13 + 2, lambda: pe.wait_ge(S("e_y"), item * 2 + 2))
                gather(lambda half: pe.wait_ge(S("m_free"), item * 13 + (12 + half)),
                       lambda: pe.wait_ge(S("s_ready"), item + 2))
                pe.wait_ge(S("e_h"), item * 7 + 7)
                for q in range(7):
                    w = slot(14 + q).rearrange("p (k n) -> p k n", k=4)
                    for kk in range(4):
                        kf = 4 * q + kk
                        for m in nk:
                            ins = mm(psum[4 + m // 4][:, CAP * (m % 4):CAP * (m % 4) + CAP], w[:, kk, P * m:P * m + P],
                                     hE[:, kf, :], start=(kf == 0 and m % 4 == 0), stop=(kf == ET - 1),
                                     skip_group_check=True)
                    ins.then_inc(S("w_used"), 1)
            spread(n_items * 13 + 2, lambda: pe.wait_ge(S("e_y"), n_items * 2 + 2))
            norm(4, 2 * IT)
            for n in range(3):
                for half in range(2):
                    u = 2 * n + half
                    if u >= 2:
                        pe.wait_ge(S("yrow_ready"), u - 1)
                    for k in range(4):
                        m = 4 * half + k
                        if u < 2:
                            pe.wait_ge(S("a_ready"), 4 * DT + m + 1)
                        ins = tr(psum[half][0:ROWS[n], P * k:P * k + P], aT[:, m, P * n:P * n + ROWS[n]], ident[:, :])
                    ins.then_inc(S("yrow_tr"), 1)

        @block.vector
        def _(dve):
            own = Order(dve, S("dve_own"))
            tt, ts, stt = dve.tensor_tensor, dve.tensor_scalar, dve.scalar_tensor_tensor

            def step(ins):
                own.did(ins)
                own.settle()

            for m in nk:
                dve.wait_ge(S("x_tr"), m + 1)
                dve.tensor_copy(xT[:, m, :], psum[m % 2][:, 0:T]).then_inc(S("x_ready"), 1)
            dve.wait_ge(S("x_tr"), DT)
            dve.wait_ge(S("vec_ready"), 1)

            def inverse(root, bank, width):
                ts(rs[:, 0, :], psum[bank][:, 0:T], 1.0 / width, EPS, ALU.mult, ALU.add).then_inc(S(root[0]), 1)
                dve.wait_ge(S(root[1]), root[2])
                step(dve.reciprocal(rs[:, 0, :], rs[:, 1, :]))

            def norm(n, before_):
                dve.wait_ge(S("sq_used"), DT * (n + 1) + before_)
                inverse(("ms_ready", "root_ready", n + 1), 7, D)
                for m in nk:
                    c = NORM[n] + m
                    stt(out=aT[:, m, :], in0=xT[:, m, :], scalar=V[:, c:c + 1], in1=rs[:, 0, :],
                        op0=ALU.mult, op1=ALU.mult).then_inc(S("a_ready"), 1)

            dve.memset(raw[:, 0, 0:3], 0.0).then_inc(S("pads"), 1)
            dve.memset(raw[:, 1, 0:3], 0.0).then_inc(S("pads"), 1)
            dve.wait_ge(S("pads"), 2)
            for half in range(2):
                dve.wait_ge(S("crow_tr"), half + 1)
                dve.tensor_copy(convS[:, 12 * half:12 * half + 12, :, 0:3],
                                psum[5 + half][:, 0:288].rearrange("p (t b k) -> p t b k", t=12, b=NS)
                                ).then_inc(S("convS_ready"), 1)
            dve.wait_ge(S("convS_ready"), 2)
            norm(0, 0)
            dve.wait_ge(S("vec_tr"), 1)
            dve.nop().then_inc(S("start_over"), 1)
            dve.wait_ge(S("dtw_in"), 32)
            dve.wait_ge(S("dt_mm"), 1)
            step(ts(dtT, psum[6][0:H, 0:T], dtb, None, ALU.add))
            step(stt(out=dtw, in0=dtT, scalar=-1.0, in1=dtT, op0=ALU.mult, op1=ALU.max))
            dve.nop().then_inc(S("dt_abs"), 1)
            dve.wait_ge(S("a_exp"), 1)
            step(ts(aneg, aneg, -1.0, None, ALU.mult))

            def conv(n):
                t = XO[n]
                dve.wait_ge(S("raw_ready"), 2 * n + 2)
                u = raw[:, n % 2, :]
                cw = [V[:, CW + CT * k + t:CW + CT * k + t + 1] for k in range(4)]
                out = xbc[:, t, 0:NP_]
                own.did(ts(cs1, u[:, 0:256], cw[0], None, ALU.mult))
                own.did(tt(cprod, convS[:, t],
                           V[:, CW + t:CW + t + 3 * CT + 1:CT].unsqueeze(1).to_broadcast((P, NS, 4)), ALU.mult))
                own.settle()
                own.did(stt(out=cs1, in0=u[:, 1:257], scalar=cw[1], in1=cs1, op0=ALU.mult, op1=ALU.add))
                own.did(dve.tensor_reduce(xbc[:, t, NP_:T], cprod, AX, ALU.add))
                own.settle()
                step(stt(out=cs1, in0=u[:, 2:258], scalar=cw[2], in1=cs1, op0=ALU.mult, op1=ALU.add))
                own.did(dve.tensor_copy(tail[:, t, 0:3], u[:, 256:259]))
                own.did(dve.tensor_copy(tail[:, t, 3:11], convS[:, t, :, 3]))
                own.did(stt(out=out, in0=u[:, 3:259], scalar=cw[3], in1=cs1, op0=ALU.mult, op1=ALU.add))
                own.settle()
                dve.nop().then_inc(S("conv_done"), 1)

            def xdt(q):
                dve.wait_ge(S("xtr"), q + 1)
                tt(Xdt[:, :, P * q:P * q + P].rearrange("p c (h d) -> p c h d", h=2),
                   psum[2 + q % 2][:, 0:256].rearrange("p (c h d) -> p c h d", c=2, h=2),
                   dtk_v[:, 0, :, 2 * q:2 * q + 2].unsqueeze(3).to_broadcast((P, 2, 2, 64)),
                   ALU.mult).then_inc(S("xdt_ready"), 1)

            for n in range(CT):
                conv(n)
                if n == 4:
                    dve.wait_ge(S("dt_log"), 1)
                    step(stt(out=dtT, in0=dtT, scalar=0.0, in1=dtw, op0=ALU.max, op1=ALU.add))
                    own.did(ts(dtv, dtT, aneg, None, ALU.mult))
                    own.did(dve.memset(laraw, 1.0))
                    own.settle()
                    for c in range(2):
                        own.did(dve.tensor_tensor_scan(LAT[:, P * c:P * c + P], laraw[:, P * c:P * c + P],
                                                       dtv[:, P * c:P * c + P], 0.0, ALU.mult, ALU.add))
                    own.did(dve.tensor_copy(dsx[:, 0:8], dtT[:, NP_:T]))
                    own.did(dve.tensor_copy(dsx[:, 8:16], dtv[:, NP_:T]))
                    own.settle()
                    for c in range(2):
                        own.did(ts(dle[:, H * c:H * c + H], ident[0:H, 0:H], LAT[:, P * c + 127:P * c + 128], None, ALU.mult))
                    own.settle()
                    dve.nop().then_inc(S("dsx_dt"), 1)
                    dve.nop().then_inc(S("dt_ready"), 1)
                if n == 8:
                    dve.wait_ge(S("dtk_tr"), 1)
                    step(dve.tensor_copy(dtk, psum[6][:, 0:P]))
                    le = psum[6][:, P:P + 64]
                    own.did(tt(wend[:, 0, :], le[:, 0:H], dtk_v[:, 1, 0, :], ALU.subtract))
                    own.did(tt(wend[:, 2, :], le[:, H:2 * H], dtk_v[:, 1, 1, :], ALU.subtract))
                    own.settle()
                    step(tt(wend[:, 1, :], le[:, H:2 * H], wend[:, 0, :], ALU.add))
                    dve.nop().then_inc(S("dtk_ready"), 1)
                    dve.nop().then_inc(S("wend_in"), 1)
                    idh = ident[0:H, 0:H]
                    own.did(dve.tensor_reduce(hsel, idh.rearrange("p (t w) -> p w t", w=2), AX, ALU.add))
                    own.did(dve.tensor_reduce(psel, idh.rearrange("p (t w) -> p t w", w=2), AX, ALU.add))
                    own.settle()
                    own.did(dve.tensor_copy(halves.rearrange("p (w q) -> p w q", w=2),
                                            hsel.unsqueeze(2).to_broadcast((H, 2, 64))))
                    dve.wait_ge(S("dsx_ready"), 1)
                    own.did(tt(dspr.rearrange("p (t n) -> p t n", t=IT), dsx.unsqueeze(1).to_broadcast((H, IT, 16)),
                               psel.unsqueeze(2).to_broadcast((H, IT, 16)), ALU.mult))
                    own.settle()
                    dve.nop().then_inc(S("spread_ready"), 1)
                if n == 9:
                    dve.wait_ge(S("sexp_mm"), 1)
                    dve.tensor_copy(sexp, psum[6][:, 256:512].rearrange("p (t w b) -> p t w b", t=IT, w=2)
                                    ).then_inc(S("sexp_ready"), 1)
                    dve.nop().then_inc(S("sexp_ready"), 1)
                if n == 10:
                    for half in range(2):
                        dve.wait_ge(S("cb"), half + 1)
                        tt(CBm[:, 2 * half:2 * half + 2].rearrange("p g c i -> p (g c) i"),
                           psum[2 + half][:, :].rearrange("p (a i) -> p a i", a=4),
                           causal[:, :].unsqueeze(1).to_broadcast((P, 4, P)), ALU.mult).then_inc(S("cbm_ready"), 1)
                if n >= 13:
                    xdt(n - 13)
            dve.nop().then_inc(S("tail_ready"), 1)
            for q in range(11, IT):
                xdt(q)
            dve.wait_ge(S("xbc_ready"), CT)
            dve.wait_ge(S("sexp_ready"), 2)
            step(tt(dtx, xbc[:, 0:IT, NP_:T], sexp[:, :, 0, :], ALU.mult))
            dve.wait_ge(S("cols_in"), 64)
            dve.wait_ge(S("cbm_ready"), 2)

            def y_out(u):
                dve.wait_ge(S("y_mm"), u + 1)
                stt(out=xbc[:, u, 0:NP_], in0=xbc[:, u, 0:NP_], scalar=dcol[:, u:u + 1], in1=psum[4][:, 0:256],
                    op0=ALU.mult, op1=ALU.add).then_inc(S("y_done"), 1)

            for t in range(IT):
                g = t // 4
                dve.wait_ge(S("la"), t + 1)
                if t:
                    dve.wait_ge(S("ex_ready"), t)
                la = psum[2 + t % 2][:, :].rearrange("p (h c i) -> p h c i", h=2, c=2)
                for h in range(2):
                    for c in range(2):
                        k = 2 * t + h
                        ins = ts(seg[:, h, c, :], la[:, h, c, :], dtk_v[:, 1, c, k:k + 1], 0.0, ALU.subtract, ALU.min)
                        own.did(ins)
                own.settle()
                dve.nop().then_inc(S("seg_ready"), 1)
                dve.wait_ge(S("el_ready"), t + 1)
                if t >= 2:
                    dve.wait_ge(S("y_mm"), t - 1)
                tt(ce[:, t % 2], el, xbc[:, 20 + g, P:2 * P].unsqueeze(1).to_broadcast((P, 2, P)),
                   ALU.mult).then_inc(S("ce_ready"), 1)
                dve.wait_ge(S("ex_ready"), t + 1)
                tt(mm_[:, t % 2].rearrange("p h c i -> p h (c i)"), ex.rearrange("p h c i -> p h (c i)"),
                   CBm[:, g].rearrange("p c i -> p (c i)").unsqueeze(1).to_broadcast((P, 2, 256)),
                   ALU.mult).then_inc(S("m_ready"), 1)
                if t % 4 == 0:
                    dve.wait_ge(S("misc_free"), 4 + 6 * g + 6)
                for b in range(NS):
                    n = NS * t + b
                    dve.wait_ge(S("decayed"), n + 1)
                    stt(out=st[:, t % SB, b, :], in0=sbc[:, 0, b, :], scalar=dtx[:, t, b:b + 1], in1=hd[:, n % 2, :],
                        op0=ALU.mult, op1=ALU.add).then_inc(S("upd"), 1)
                for b in range(NS):
                    dve.wait_ge(S("upd"), NS * t + b + 1)
                    own.settle(1)
                    own.did(dve.tensor_tensor_reduce(junk[:, b % 2], st[:, t % SB, b, :], sbc[:, 1, b, :], 1.0, 0.0,
                                                     ALU.mult, ALU.add, ys[:, b:b + 1]))
                own.settle()
                step(stt(out=xbc[:, t, NP_:T], in0=xbc[:, t, NP_:T], scalar=dcol[:, t:t + 1], in1=ys,
                         op0=ALU.mult, op1=ALU.add))
                dve.nop().then_inc(S("y_sample"), 1)
                if t:
                    y_out(t - 1)
            y_out(IT - 1)
            dve.wait_ge(S("y_done"), IT)
            for t in range(IT):
                dve.wait_ge(S("gate_ready"), t // 4 + 1)
                tt(zT[:, t, :], zT[:, t, :], xbc[:, t, :], ALU.mult).then_inc(S("gated"), 1)
            for q in range(6):
                u = 28 + q
                dve.wait_ge(S("misc"), u + 1)
                dve.tensor_copy(ncv[:, 512 * q:512 * q + 512], psum[5 + u % 2][0:11, :]).then_inc(S("misc_free"), 1)
            dve.wait_ge(S("misc_free"), 34)
            dve.nop().then_inc(S("ncv_ready"), 1)
            for g in range(G):
                dve.wait_ge(S("sq_used"), DT + 4 * g + 4)
                if g:
                    dve.wait_ge(S("yg_ready"), 4 * g)
                inverse(("gms_ready", "groot_ready", g + 1), 7, DI // G)
                for k in range(4):
                    n = 4 * g + k
                    ins = stt(out=zT[:, n, :], in0=zT[:, n, :], scalar=V[:, GN + n:GN + n + 1], in1=rs[:, 0, :],
                              op0=ALU.mult, op1=ALU.mult)
                    ins.then_inc(S("yg_ready"), 1)
            dve.nop().then_inc(S("ssd_over"), 1)

            def residual(n):
                for m in nk:
                    dve.wait_ge(S("o_mm"), DT * (n - 1) + m + 1)
                    tt(xT[:, m, :], xT[:, m, :], psum[m % 2][:, 0:T], ALU.add).then_inc(S("x_ready"), 1)
                dve.wait_ge(S("x_ready"), DT * (n + 1))

            residual(1)
            norm(1, IT)
            for n in range(FT):
                dve.wait_ge(S("ffn_silu"), n + 1)
                tt(hT[:, n, :], fs[:, n % 2, :], psum[2 * (n % 2) + 1][:, 0:T], ALU.mult).then_inc(S("ffn_h"), 1)
            residual(2)
            norm(2, IT)
            for half in range(2):
                dve.wait_ge(S("ws_tr"), half + 1)
                tt(wsT[:, 4 * half:4 * half + 4, :], psum[4 + half][:, :].rearrange("p (g i) -> p g i", g=4),
                   causal[:, :].unsqueeze(1).to_broadcast((P, 4, P)), ALU.mult).then_inc(S("wsT_ready"), 1)
            dve.wait_ge(S("v_sum"), 1)
            step(ts(mus, psum[7][:, 0:T], -1.0 / DI, None, ALU.mult))
            for t in range(IT):
                dve.wait_ge(S("gelu"), t + 1)
                tt(vT[:, t, :], vT[:, t, :], mus, ALU.add).then_inc(S("v_centred"), 1)
            dve.wait_ge(S("v_centred"), IT)
            dve.wait_ge(S("sq_used"), 3 * DT + 2 * IT)
            inverse(("vms_ready", "vroot_ready", 1), 6, DI)
            for t in range(IT):
                own.did(stt(out=vT[:, t, :], in0=vT[:, t, :], scalar=V[:, LG + t:LG + t + 1], in1=rs[:, 0, :],
                            op0=ALU.mult, op1=ALU.mult))
                own.settle()
                ts(vT[:, t, :], vT[:, t, :], V[:, LB + t:LB + t + 1], None, ALU.add).then_inc(S("vn_ready"), 1)
                if t:
                    dve.wait_ge(S("vtr"), t)
                    dve.tensor_copy(vtok[:, :, P * (t - 1):P * t],
                                    psum[4 + (t - 1) % 2][:, 0:256].rearrange("p (c d) -> p c d", c=2)).then_inc(S("vtok_ready"), 1)
            dve.wait_ge(S("vtr"), IT)
            dve.tensor_copy(vtok[:, :, P * 15:P * 16],
                            psum[5][:, 0:256].rearrange("p (c d) -> p c d", c=2)).then_inc(S("vtok_ready"), 1)
            dve.wait_ge(S("gelu"), 2 * IT)
            for t in range(IT):
                g = t // 2
                dve.wait_ge(S("vn_ready"), t + 1)
                step(ts(ssm[:, 0, :], vT[:, t, NP_:T], w00[:, g:g + 1], b00[:, g:g + 1], ALU.mult, ALU.add))
                own.did(tt(uT[:, t, NP_:T], uT[:, t, NP_:T], ssm[:, 0, :], ALU.mult))
                dve.wait_ge(S("sp_mm"), t + 1)
                own.did(tt(uT[:, t, 0:NP_], uT[:, t, 0:NP_], psum[2 + t % 2][:, 0:256], ALU.mult))
                own.settle()
                dve.nop().then_inc(S("sp_done"), 1)
            for q in range(4):
                dve.wait_ge(S("vnew_tr"), q + 1)
                dve.tensor_copy(vnew[:, 512 * q:512 * q + 512], psum[6][0:NS, :]).then_inc(S("vnew_ready"), 1)
            residual(3)
            norm(3, 2 * IT)

            dve.wait_ge(S("v_out"), 16)
            dve.wait_ge(S("iota"), 1)
            own.did(dve.tensor_copy(iota, ioti[:, :]))
            own.did(dve.memset(L, 0.0))
            own.did(dve.memset(valid, 1.0))
            own.did(dve.memset(SG, 0.0))
            own.did(dve.memset(incl, 1.0))
            own.settle()
            own.did(dve.memset(valid[:, 2:3], 0.0))
            own.did(ts(rev, iota[:, 0:E], -1.0, float(E), ALU.mult, ALU.add))
            for k in range(MORE // E):
                own.did(dve.tensor_copy(ev[:, E * k:E * k + E], iota[:, 0:E]))
            dve.wait_ge(S("logits"), 1)
            own.did(dve.tensor_copy(L[:, 0:2, :], psum[4][:, 0:16].rearrange("p (n e) -> p n e", n=2)))
            own.did(dve.tensor_copy(L[0:NS, 2, :], psum[4][0:NS, 16:24]))
            own.settle()
            step(dve.memset(valid[0:NS, 2:3], 1.0))
            wide = (P, 3, E)

            def first_max(src, m, oh):
                step(dve.tensor_reduce(m, src, AX, ALU.max))
                step(tt(eq, src, m.unsqueeze(2).to_broadcast(wide), ALU.is_equal))
                step(tt(eq, eq, rev.unsqueeze(1).to_broadcast(wide), ALU.mult))
                step(dve.tensor_reduce(mx, eq, AX, ALU.max))
                step(tt(oh, eq, mx.unsqueeze(2).to_broadcast(wide), ALU.is_equal))

            first_max(L, m1, oh1)
            step(stt(out=L2, in0=oh1, scalar=-3.0e38, in1=L, op0=ALU.mult, op1=ALU.add))
            first_max(L2, m2, oh2)
            own.did(tt(ed, m2, m1, ALU.subtract))
            own.did(tt(msk, oh1, oh2, ALU.add))
            own.settle()
            dve.nop().then_inc(S("diff_ready"), 1)
            step(tt(msk, msk, valid.unsqueeze(2).to_broadcast(wide), ALU.mult))
            dve.nop().then_inc(S("mask_ready"), 1)
            for u in range(6):
                n, half = u // 2, u % 2
                dve.wait_ge(S("atok_tr"), u + 1)
                dve.tensor_copy(atok[0:ROWS[n], n, 512 * half:512 * half + 512], psum[half][0:ROWS[n], :]).then_inc(S("atok_ready"), 1)
            dve.wait_ge(S("ediff_ready"), 1)
            step(ts(den, ed, 1.0, None, ALU.add))
            step(dve.reciprocal(g1, den))
            step(tt(g2, ed, g1, ALU.mult))
            own.did(tt(gw, oh1, g1.unsqueeze(2).to_broadcast(wide), ALU.mult))
            own.did(tt(eq, oh2, g2.unsqueeze(2).to_broadcast(wide), ALU.mult))
            own.settle()
            step(tt(gw, gw, eq, ALU.add))
            for k in range(MORE // E):
                own.did(dve.tensor_copy(gw2[:, :, E * k:E * k + E], gw))
            own.did(dve.tensor_copy(Gall[:, :, 0:E], gw))
            dve.wait_ge(S("ranks"), 1)
            rk = psum[5][:, 0:24].rearrange("p (n e) -> p n e", n=3)
            for k in range(CHUNKS):
                step(ts(pos, rk, FAR - CAP * k, None, ALU.add))
                step(tt(pos, pos, msk, ALU.mult))
                step(ts(Q[:, :, E * k:E * k + E], pos, -FAR, None, ALU.add))
            own.did(dve.tensor_copy(Aall[:, :, 0:E], Q[:, :, 0:E]))
            for k in range(1, CHUNKS):
                own.did(ts(pres[:, E * (k - 1):E * k], psum[5][:, 24:32], float(CAP * k) + 0.5, None, ALU.is_gt))
            own.settle()
            step(dve.tensor_tensor_scan(OX[:, 0, :], incl, pres, float(E), ALU.mult, ALU.add))
            own.did(tt(incl, OX[:, 0, :], pres, ALU.mult))
            own.did(dve.tensor_copy(iti[0:1, ITEMS:ITEMS + 1], OX[0:1, 0, MORE - 1:MORE]))
            own.settle()
            step(ts(incl, incl, -1.0, None, ALU.add))
            jw = (P, MORE + 1, MORE)
            step(tt(OJ, iota[:, E:E + MORE + 1].unsqueeze(2).to_broadcast(jw), incl.unsqueeze(1).to_broadcast(jw), ALU.is_equal))
            own.did(dve.tensor_copy(itf[:, 0:E], iota[:, 0:E]))
            for src, dst in [(ev, itf[:, E:ITEMS])] + [(Q[:, n, E:E + MORE], Aall[:, n, E:ITEMS]) for n in range(3)] \
                    + [(gw2[:, n, :], Gall[:, n, E:ITEMS]) for n in range(3)]:
                step(tt(OX, OJ, src.unsqueeze(1).to_broadcast(jw), ALU.mult))
                step(dve.tensor_reduce(dst, OX, AX, ALU.add))
            step(dve.tensor_copy(iti[0:1, 0:ITEMS], itf[0:1, :]))
            own.did(dve.memset(ye, 0.0)) 
            own.settle()

            def chosen(j):
                for n in range(3):
                    ins = ts(Sm[:, n, :], iota[:, 0:CAP], Aall[:, n, bass.ds(j, 1)], None, ALU.is_equal)
                    own.did(ins)

            chosen(0)
            own.settle()
            dve.nop().then_inc(S("s_ready"), 1)
            dve.nop().then_inc(S("e_y"), 2)
            dve.nop().then_inc(S("items_ready"), 1)
            n_items = dve.value_load(iti[0:1, ITEMS:ITEMS + 1], min_val=E, max_val=E + MORE)

            def gathered(mbase):
                for half in range(2):
                    dve.wait_ge(S("m_mm"), mbase + half)
                    own.did(dve.tensor_copy(xe[:, 4 * half:4 * half + 4, :],
                                            psum[7 - half][:, 0:4 * CAP].rearrange("p (m c) -> p m c", m=4)))
                    own.settle()
                    dve.nop().then_inc(S("m_free"), 1)
                    dve.nop().then_inc(S("xe_ready"), 1)

            def spread(mbase):
                dve.wait_ge(S("m_mm"), mbase)
                dve.tensor_copy(GT, psum[6][0:CAP, 0:T]).then_inc(S("m_free"), 1)
                for half in range(2):
                    dve.wait_ge(S("m_mm"), mbase + 1 + half)
                    dve.tensor_copy(yt[:, 512 * half:512 * half + 512], psum[7 - half][0:CAP, :]).then_inc(S("m_free"), 1)
                for m in nk:
                    dve.wait_ge(S("m_mm"), mbase + 3 + m)
                    tt(xT[:, m, :], xT[:, m, :], psum[7 - m % 2][:, 0:T], ALU.add).then_inc(S("m_free"), 1)

            gathered(1)
            before_loop = own.n
            STEPS = 8
            with dve.Fori(0, n_items) as item:
                own.base, own.n = item * STEPS + before_loop, 0
                for j in range(7):
                    dve.wait_ge(S("e_silu"), item * 7 + (j + 1))
                    tt(hE[:, 4 * j:4 * j + 4, :].rearrange("p m c -> p (m c)"), es[:, j % 2, :],
                       psum[2 * (j % 2) + 1][:, 0:4 * CAP], ALU.mult).then_inc(S("e_h"), 1)
                    if j == 1:
                        spread(item * 13 + 3)
                        for n in range(3):
                            own.did(ts(SG[:, n, :], iota[:, 0:CAP], Aall[:, n, bass.ds(item, 1)],
                                       Gall[:, n, bass.ds(item, 1)], ALU.is_equal, ALU.mult))
                        chosen(item + 1)
                        own.settle()
                        dve.nop().then_inc(S("s_ready"), 1)
                gathered(item * 13 + 14)
                assert own.n == STEPS, own.n
            own.base, own.n = n_items * STEPS + before_loop, 0
            spread(n_items * 13 + 3)
            dve.wait_ge(S("m_free"), n_items * 13 + 13)
            dve.nop().then_inc(S("x_ready"), DT)
            norm(4, 2 * IT)
            for u in range(6):
                n, half = u // 2, u % 2
                dve.wait_ge(S("yrow_tr"), u + 1)
                dve.tensor_copy(yrow[0:ROWS[n], n, 512 * half:512 * half + 512], psum[half][0:ROWS[n], :]).then_inc(S("yrow_ready"), 1)
            dve.wait_ge(S("yrow_ready"), 6)
            dve.nop().then_inc(S("y_stored"), 1)


_OUTS = [(1, 256, 1024), (8, 1, 1024), (1, 1, 32, 64, 128), (1, 1, 3, 3072), (1, 8, 32, 64, 128), (1, 8, 3, 3072), (1, 8, 1, 2048)]
_INS = ["x_prompt", "x_sample", "state_ssm", "state_conv", "norm_mix", "norm_ffn", "norm_final",
        "ssd_w_in", "ssd_conv_w", "ssd_conv_b", "ssd_dt_bias", "ssd_a_log", "ssd_d", "ssd_gnorm", "ssd_w_out",
        "sgu_w_in", "sgu_b_in", "sgu_ln_g", "sgu_ln_b", "sgu_w_s", "sgu_b_s", "sgu_w_out",
        "ffn_w_gu", "ffn_w_down", "moe_w_router", "moe_w_gu", "moe_w_down"]


def kernel(**inputs):
    import numpy as _np
    import concourse.bacc as _bacc
    from concourse import mybir as _mybir
    from concourse.bass_utils import run_bass_kernel_spmd as _run

    nc = _bacc.Bacc("TRN2", target_bir_lowering=False, num_devices=1)
    arrays, ins = {}, {}
    for name in _INS:
        a = _np.ascontiguousarray(inputs[name])
        arrays[f"in_{name}_dram"] = a
        ins[name] = nc.dram_tensor(f"in_{name}_dram", a.shape, _mybir.dt.from_np(a.dtype), kind="ExternalInput").ap()
    outs = [nc.dram_tensor(f"out_{n}_dram", s, _mybir.dt.float32, kind="ExternalOutput").ap() for n, s in enumerate(_OUTS)]
    hybrid_step(nc, ins, outs)
    r = _run(nc, [arrays], core_ids=[0])
    return tuple(r.results[0][f"out_{n}_dram"] for n in range(len(_OUTS)))
```

```python
from contextlib import ExitStack

import concourse.bass as bass
from concourse import mybir

F32 = mybir.dt.float32
F32R = mybir.dt.float32r
I32 = mybir.dt.int32
ALU = mybir.AluOpType
ACT = mybir.ActivationFunctionType
AX = mybir.AxisListType.X

P = 128
D = 1024
DT = D // P
NP_ = 256
NS = 8
T = NP_ + NS
ROWS = [P, P, NS]
DI = 2048
IT = DI // P
H = 32
G = 4
CD = 3072
CT = CD // P
FF = 2816
FT = FF // P
E = 8
FE = 3584
ET = FE // P
CAP = 128
CHUNKS = -(-T // CAP)
MORE = E * (CHUNKS - 1)
ITEMS = E + MORE + 1
SLOT = 2048
RAW = 8
RING = 7
SSD_RING = 2
SHARE = 1536
PARTS = 3
ETILES = 42
SB = 3
HB = 4
EPS = 1e-5
FAR = 10000.0


class Order:

    def __init__(self, eng, sem):
        self.eng, self.sem, self.n, self.base = eng, sem, 0, 0

    def did(self, ins):
        ins.then_inc(self.sem, 1)
        self.n += 1

    def settle(self, but=0):
        self.eng.wait_ge(self.sem, self.base + (self.n - but))


def hybrid_step(nc, i, o):
    ctx = ExitStack()
    with ctx:
        sems = {}

        def S(name):
            if name not in sems:
                sems[name] = ctx.enter_context(nc.semaphore(name))
            return sems[name]

        def sb(name, shape, dt=F32):
            return ctx.enter_context(nc.sbuf_tensor(name, shape, dt))

        raw_w = sb("raw_w", [P, RAW, SLOT])
        part = sb("part", [P, PARTS, 2, SLOT], F32R)
        xT = sb("xT", [P, DT, T])
        sq = sb("sq", [P, 2, T])
        rs = sb("rs", [P, 2, T])
        ident = sb("ident", [P, P])
        ones = sb("ones", [P, P])
        causal = sb("causal", [P, P])
        before = sb("before", [P, P])
        V = sb("V", [P, 240])
        small = sb("small", [P, 64])
        iti = sb("iti", [1, ITEMS + 1], I32)
        ioti = sb("ioti", [P, P], I32)
        psum = [ctx.enter_context(nc.psum_tensor(f"bank{b}", [P, 512], F32)) for b in range(8)]

        BASE = nc.sbuf_base
        A_AT, AHL_AT, ARENA_AT = BASE, BASE + 8448, BASE + 8448 + 16896
        END = nc.sbuf_usable_end
        slot7 = raw_w[:, 7, :]

        def at(name, shape, offset, dt=F32):
            n = 4
            for k in shape[1:]:
                n *= k
            assert offset + n <= END, (name, offset + n, END)
            return nc.alloc_sbuf_tensor_at(name, shape, dt, offset=offset)

        aT = at("aT", [P, DT, T], A_AT)
        ah = at("ah", [P, DT, T], AHL_AT, F32R)
        al = at("al", [P, DT, T], AHL_AT + 8448, F32R)
        ARENA = (END - ARENA_AT) // 4
        arena = at("arena", [P, ARENA], ARENA_AT)
        scratch = at("scratch", [P, 2048], A_AT)

        class Room:

            def __init__(self, ap, size, at=0):
                self.ap, self.size, self.at = ap, size, at

            def take(self, n):
                self.at += n
                assert self.at <= self.size, (self.at, self.size)
                return self.ap[:, self.at - n:self.at]

        NM = [0, 8]
        NF = [16, 24]
        NFIN, GN, CB_, LG, LB = 32, 40, 56, 80, 96
        CW, BI = 112, 208
        NORM = [NM[0], NF[0], NM[1], NF[1], NFIN]
        dcol = small[:, 0:16]
        w00 = small[:, 16:24]
        b00 = small[:, 24:32]
        dtb = small[0:H, 32:33]
        alog = small[0:H, 33:34]
        aneg = small[0:H, 34:35]

        r = Room(arena, ARENA)
        zT = r.take(IT * T).rearrange("p (t n) -> p t n", t=IT)
        xbc = r.take(CT * T).rearrange("p (t n) -> p t n", t=CT)
        e_ = Room(zT.rearrange("p t n -> p (t n)"), IT * T)
        convS = e_.take(CT * NS * 4).rearrange("p (t b k) -> p t b k", t=CT, b=NS)
        raw = e_.take(2 * 259).rearrange("p (u n) -> p u n", u=2)
        wdt = e_.take(DT * H).rearrange("p (k n) -> p k n", k=DT)
        cs1 = e_.take(256)
        cprod = e_.take(NS * 4).rearrange("p (b k) -> p b k", b=NS)
        l_ = Room(xbc[:, 16:20, :].rearrange("p t n -> p (t n)"), 4 * T)
        fin = l_.take(512)
        ce = l_.take(512).rearrange("p (u h i) -> p u h i", u=2, h=2)
        q_ = Room(sq[:, :, :].rearrange("p u n -> p (u n)"), 2 * T)
        hd = q_.take(HB * P).rearrange("p (u n) -> p u n", u=HB)
        el = r.take(256).rearrange("p (h i) -> p h i", h=2)
        tail = r.take(CT * 11).rearrange("p (t k) -> p t k", t=CT)
        seg = r.take(512).rearrange("p (h c i) -> p h c i", h=2, c=2)
        ex = seg
        mm_ = r.take(1024).rearrange("p (u h c i) -> p u h c i", u=2, h=2, c=2)
        hp = scratch[:, 0:512]
        xsf = scratch[:, 512:2048].rearrange("p (k n) -> p k n", k=3)
        dtk = r.take(P)
        dtk_v = dtk.rearrange("p (w c h) -> p w c h", w=2, c=2)
        wend = r.take(96).rearrange("p (k h) -> p k h", k=3)
        sexp = r.take(256).rearrange("p (t w b) -> p t w b", t=IT, w=2)
        dtx = r.take(P).rearrange("p (t b) -> p t b", t=IT)
        ys = r.take(NS)
        junk = r.take(2 * P).rearrange("p (u n) -> p u n", u=2)
        dtT = xsf[0:H, 0, 0:T]
        dtw = xsf[0:H, 1, 0:T]
        dtv = xsf[0:H, 2, 0:T]
        LAT = r.take(256)[0:H, :]
        laraw = hp[0:H, 0:256]
        dspr = hp[0:H, 256:512]
        halves = xsf[0:H, 0, 384:512]
        hsel = xsf[0:H, 1, 384:386]
        psel = xsf[0:H, 1, 400:416]
        dle = r.take(64)[0:H, :]
        dsx = r.take(16)[0:H, :]
        zh = at("zh", [P, IT, T], ARENA_AT + 4 * IT * T, F32R)
        zl = at("zl", [P, IT, T], ARENA_AT, F32R)
        s = Room(raw_w[:, SSD_RING:RAW, :].rearrange("p r n -> p (r n)"), (RAW - SSD_RING) * SLOT)
        Xdt = s.take(2 * DI).rearrange("p (c n) -> p c n", c=2)
        st = s.take(SB * 1024).rearrange("p (u b n) -> p u b n", u=SB, b=NS)
        bcs = s.take(1024)[0:NS, :]
        sbc = s.take(2 * 1024).rearrange("p (w b n) -> p w b n", w=2, b=NS)
        Btok = s.take(1024).rearrange("p (c n) -> p c n", c=2)
        CBm = s.take(1024).rearrange("p (g c i) -> p g c i", g=G, c=2)
        xtok = s.ap[:, 0:3072].rearrange("p (n d) -> p n d", n=3)
        vrow = s.ap[:, 4096:4352].rearrange("p (u d) -> p u d", u=2)
        crow = s.ap[0:24, 5120:8192]
        ncv = s.ap[0:11, 8192:8192 + 3072]

        hh = at("hh", [P, FT, T], ARENA_AT, F32R)
        hl = at("hl", [P, FT, T], ARENA_AT + 4 * FT * T, F32R)
        r = Room(arena, ARENA, 2 * FT * T)
        fs = r.take(2 * T).rearrange("p (u n) -> p u n", u=2)
        hf = r.take(2 * T).rearrange("p (u n) -> p u n", u=2)
        r = Room(arena, ARENA)
        uT = r.take(IT * T).rearrange("p (t n) -> p t n", t=IT)
        vT = r.take(IT * T).rearrange("p (t n) -> p t n", t=IT)
        vtok = r.take(2 * DI).rearrange("p (c n) -> p c n", c=2)
        wsT = r.take(8 * P).rearrange("p (g i) -> p g i", g=8)
        r = Room(slot7, SLOT)
        wsr = r.take(8 * P).rearrange("p (g j) -> p g j", g=8)
        bsr = r.take(P)[0:8, :]
        mus = r.take(T)
        ssm = r.take(2 * NS).rearrange("p (u n) -> p u n", u=2)
        vnew = scratch[0:NS, :]
        uh = at("uh", [P, IT, T], ARENA_AT + 4 * IT * T, F32R)
        ul = at("ul", [P, IT, T], ARENA_AT, F32R)
        hEh = at("hEh", [P, ET, CAP], ARENA_AT, F32R)
        hEl = at("hEl", [P, ET, CAP], ARENA_AT + 4 * ET * CAP, F32R)
        r = Room(arena, ARENA, 2 * ET * CAP)
        atok = r.take(3 * D).rearrange("p (n d) -> p n d", n=3)
        es = slot7[:, 0:1024].rearrange("p (u n) -> p u n", u=2)
        hx = slot7[:, 1024:2048].rearrange("p (u n) -> p u n", u=2)
        xh = at("xh", [P, DT, CAP], AHL_AT, F32R)
        xl = at("xl", [P, DT, CAP], AHL_AT + 4 * DT * CAP, F32R)
        moe2 = at("moe2", [P, 2056], AHL_AT + 8 * DT * CAP)
        r2 = Room(moe2, 2056)
        yt = r2.take(D)
        GT = r2.take(T)
        Sm = r2.take(3 * CAP).rearrange("p (n c) -> p n c", n=3)
        SG = r2.take(3 * CAP).rearrange("p (n c) -> p n c", n=3)
        iota = r.take(P)
        wr = r.take(DT * E).rearrange("p (k e) -> p k e", k=DT)
        t38 = [r.take(24).rearrange("p (n e) -> p n e", n=3) for _ in range(8)]
        L, eq, oh1, oh2, L2, gw, msk, pos = t38
        t3 = [r.take(3) for _ in range(8)]
        m1, mx, m2, ed, den, g1, g2, valid = t3
        rev = r.take(E)
        ev = r.take(MORE)
        pres = r.take(MORE)
        incl = r.take(MORE)
        Q = r.take(3 * (E + MORE)).rearrange("p (n s) -> p n s", n=3)
        gw2 = r.take(3 * MORE).rearrange("p (n s) -> p n s", n=3)
        OJ = r.take((MORE + 1) * MORE).rearrange("p (j s) -> p j s", s=MORE)
        OX = r.take((MORE + 1) * MORE).rearrange("p (j s) -> p j s", s=MORE)
        Aall = r.take(3 * ITEMS).rearrange("p (n j) -> p n j", n=3)
        Gall = r.take(3 * ITEMS).rearrange("p (n j) -> p n j", n=3)
        itf = r.take(ITEMS)
        yrow = arena[:, 0:3072].rearrange("p (n d) -> p n d", n=3)

        w_in = i["ssd_w_in"][0].rearrange("(k p) n -> p k n", p=P)
        dense = []

        def cols(w, kt, c0, width):
            return w.rearrange("(k p) n -> p k n", p=P)[:, :, c0:c0 + width], kt, width

        XO = [16, 17, 18, 19, 20, 21, 22, 23] + list(range(16))
        for c in list(range(16, 20)) + list(range(8, 16)) + list(range(8)):
            dense.append(cols(i["ssd_w_in"][0], DT, 256 * c, 256))
        for c in range(8):
            dense.append(cols(i["ssd_w_out"][0], IT, 128 * c, 128))
        SSD_TILES = len(dense)
        for c in range(FT):
            dense.append((("pair", c), DT, 256))
        for c in range(2 * 8):
            w_down = i["ffn_w_down"][0].rearrange("(h k p) n -> h p k n", p=P, h=2)
            dense.append((w_down[c % 2, :, :, P * (c // 2):P * (c // 2) + P], FT // 2, P))
        for c in list(range(8, 16)) + list(range(8)):
            dense.append(cols(i["sgu_w_in"][0], DT, 256 * c, 256))
        for c in range(8):
            dense.append(cols(i["sgu_w_out"][0], IT, 128 * c, 128))
        place, landed, last = [], [0] * RING, [None] * RING
        q = 0
        for n, (src, _, _) in enumerate(dense):
            q = SSD_RING if n == SSD_TILES else q % (SSD_RING if n < SSD_TILES else RING)
            landed[q] += 32 if isinstance(src, tuple) else 16
            place.append((q, landed[q], last[q]))
            last[q] = n
            q += 1
        ND = len(dense)
        R0 = q % RING
        eslot = [((R0 + k) % RING, landed[(R0 + k) % RING] + 16 * (k // RING + 1)) for k in range(ETILES)]
        assert all(last[(R0 + k) % RING] == ND - RING + k for k in range(RING))
        assert ND % PARTS == 0 and ETILES % PARTS == 0 and ETILES % RING == 0

        def read(n):
            for first, count, name, made, base in (
                    (0, 20, "proj", lambda k: 2 * k + 2, 0), (20, 8, "o_mm", lambda k: k + 1, 0),
                    (28, 22, "ffn", lambda k: k + 1, 0), (50, 16, "o_mm", lambda k: k // 2 + 1, DT),
                    (66, 16, "sgu", lambda k: 2 * k + 2, 0), (82, 8, "o_mm", lambda k: k + 1, 2 * DT)):
                if n < first + count:
                    return S(name), base + made(n - first)

        def split_1(act, n):
            q, landed_ = place[n][:2] if n < ND else eslot[n - ND]
            size = dense[n][1] * dense[n][2] if n < ND else SLOT
            act.wait_ge(S(f"w{q}"), landed_)
            if n >= PARTS:
                act.wait_ge(*read(n - PARTS))
            act.activation(part[:, n % PARTS, 0, 0:size], raw_w[:, q, 0:size], ACT.Copy).then_inc(S("part1"), 1)

        def split_2(eng, n, pool=False):
            q = place[n][0] if n < ND else eslot[n - ND][0]
            size = dense[n][1] * dense[n][2] if n < ND else SLOT
            cut = 0 if n < SSD_TILES else size * SHARE // SLOT
            c = slice(cut, size) if pool else slice(0, cut)
            if pool and n > SSD_TILES:
                eng.wait_ge(S("part2"), n - SSD_TILES)
            eng.wait_ge(S("part1"), n + 1)
            eng.tensor_tensor(part[:, n % PARTS, 1, c], raw_w[:, q, c], part[:, n % PARTS, 0, c].bitcast(F32),
                              ALU.subtract).then_inc(S("part2_pool" if pool else "part2"), 1)

        def split_done(eng, n):
            eng.wait_ge(S("part2_pool"), n + 1)
            if n >= SSD_TILES:
                eng.wait_ge(S("part2"), n - SSD_TILES + 1)

        gu = i["moe_w_gu"][0]
        dn = i["moe_w_down"][0]

        ED = ND - SSD_TILES
        GATES, HTR, SP, GA, USES = 0, [1, 10, 11, 12, 13, 14, 17], 2, 15, 18
        block = ctx.enter_context(nc.Block())
        nk = range(DT)

        def col1(k):
            return ident[0:H, k:k + 1].to_broadcast((H, P))

        @block.sync
        def _(sp):
            sp.dma_start(xtok[:, 0:2, :], i["x_prompt"][0].rearrange("(n p) d -> p n d", p=P)).then_inc(S("x_in"), 16)
            sp.dma_start(xtok[0:NS, 2, :], i["x_sample"].rearrange("b s d -> (b s) d")).then_inc(S("x_in"), 16)
            sp.dma_start(wdt, w_in[:, :, DI + CD:DI + CD + H]).then_inc(S("wdt_in"), 16)
            for n, (src, kt, width) in enumerate(dense):
                q, _, prev = place[n]
                if prev is not None:
                    split_done(sp, prev)
                elif n >= SSD_TILES:
                    sp.wait_ge(S("ssd_over"), 1)
                    for k in range(SB):
                        sp.wait_ge(S(f"so{k}"), 16 * len(range(k, IT, SB)))
                    sp.wait_ge(S("conv_out"), 48)
                dst = raw_w[:, q, 0:kt * width].rearrange("p (k n) -> p k n", k=kt)
                if isinstance(src, tuple):
                    src = i["ffn_w_gu"][0].rearrange("(k p) (u n) -> p k u n", p=P, u=2)[
                        :, :, :, P * src[1]:P * src[1] + P]
                    for u in range(2):
                        sp.dma_start(dst[:, :, P * u:P * u + P], src[:, :, u, :]).then_inc(S(f"w{q}"), 16)
                else:
                    sp.dma_start(dst, src).then_inc(S(f"w{q}"), 16)

            def expert(e, item, count=ETILES):
                for s_ in range(count):
                    q, _ = eslot[s_]
                    before_ = 0 if item is None else item * ETILES
                    sp.wait_ge(S("part2_pool"), before_ + (ND + s_ - RING + 1 + 1))
                    if s_ < 28:
                        j, u, half = s_ // 4, s_ // 2 % 2, s_ % 2
                        c0 = 512 * j + FE * u
                        src = gu[bass.ds(e, 1), 512 * half:512 * half + 512, c0:c0 + 512].rearrange(
                            "e (k p) n -> p (e k) n", p=P)
                    else:
                        src = dn[bass.ds(e, 1), 256 * (s_ - 28):256 * (s_ - 27), :].rearrange(
                            "e (k p) n -> p (e k) n", p=P)
                    dst = raw_w[:, q, :].rearrange("p (k n) -> p k n", k=4 if s_ < 28 else 2)
                    sp.dma_start(dst, src).then_inc(S(f"w{q}"), 16)

            expert(0, None)
            with sp.Fori(1, E) as e:
                expert(e, e)
            sp.wait_ge(S("items_ready"), 1)
            n_items = sp.value_load(iti[0:1, ITEMS:ITEMS + 1], min_val=E, max_val=E + MORE)
            with sp.If(n_items > E):
                with sp.Fori(E, n_items) as item:
                    e = sp.value_load(iti[0:1, bass.ds(item, 1)], min_val=0, max_val=E - 1)
                    expert(e, item)
            expert(0, n_items, 2)
            sp.wait_ge(S("y_stored"), 1)
            sp.dma_start(o[0][0].rearrange("(n p) d -> p n d", p=P), yrow[:, 0:2, :]).then_inc(S("y_out"), 16)
            sp.dma_start(o[1].rearrange("b s d -> (b s) d"), yrow[0:NS, 2, :]).then_inc(S("y_out"), 16)
            sp.wait_ge(S("y_out"), 32)

        @block.gpsimd
        def _(pool):
            own = Order(pool, S("pool_own"))
            own.did(pool.memset(ident[:, :], 0.0))
            own.did(pool.memset(ones[:, :], 1.0))
            own.did(pool.memset(causal[:, :], 1.0))
            own.did(pool.memset(before[:, :], 1.0))
            own.settle()
            pool.affine_select(out=ident[:, :], in_=ident[:, :], compare_op=ALU.not_equal, fill=1.0, base=0,
                               pattern=[[-1, P]], channel_multiplier=1).then_inc(S("consts"), 1)
            pool.affine_select(out=causal[:, :], in_=causal[:, :], compare_op=ALU.is_ge, fill=0.0, base=0,
                               pattern=[[1, P]], channel_multiplier=-1).then_inc(S("consts"), 1)
            pool.affine_select(out=before[:, :], in_=before[:, :], compare_op=ALU.is_gt, fill=0.0, base=0,
                               pattern=[[1, P]], channel_multiplier=-1).then_inc(S("consts"), 1)
            pool.iota(ioti[:, :], pattern=[[1, P]], base=0, channel_multiplier=0).then_inc(S("iota"), 1)
            sd = i["ssd_d"].rearrange("o (t w) -> o w t", w=2)
            for w in range(2):
                pool.dma_start(dcol[64 * w:64 * w + 64, :], sd[:, w, :].to_broadcast((64, IT)), allow_slow_non_contiguous=True).then_inc(S("cols_in"), 16)
            pool.dma_start(w00, i["sgu_w_s"][:, :, 0, 0].to_broadcast((P, 8)), allow_slow_non_contiguous=True).then_inc(S("cols_in"), 16)
            pool.dma_start(b00, i["sgu_b_s"][:, :, 0].to_broadcast((P, 8)), allow_slow_non_contiguous=True).then_inc(S("cols_in"), 16)
            pool.dma_start(o[5][0, :, 0:2, :], i["state_conv"][0, :, 1:3, :]).then_inc(S("conv_out"), 16)

            h_in = i["state_ssm"][0].rearrange("b (t w) q n -> t (w q) b n", w=2)
            h_out = o[4][0].rearrange("b (t w) q n -> t (w q) b n", w=2)

            def state_in(t):
                pool.dma_start(st[:, t % SB], h_in[t]).then_inc(S(f"st{t % SB}"), 16)

            def weighted(g):
                pool.wait_ge(S("wend_ready"), 1)
                pool.wait_ge(S("xdt_ready"), 4 * g + 4)
                if g:
                    pool.wait_ge(S("misc"), 4 + 6 * (g - 1) + 2)
                for k, c in ((0, 0), (1, 0), (2, 1)):
                    pool.tensor_tensor(
                        xsf[:, k, :].rearrange("p (h q) -> p h q", q=64),
                        Xdt[:, c, 512 * g:512 * g + 512].rearrange("p (h q) -> p h q", q=64),
                        wend[:, k, 8 * g:8 * g + 8].unsqueeze(2).to_broadcast((P, 8, 64)),
                        ALU.mult).then_inc(S("weighted"), 1)

            def start_states():
                pool.wait_ge(S("start_over"), 1)
                for t in range(SB - 1):
                    state_in(t)

            for n in range(15):
                split_2(pool, n, True)
                if n == 2:
                    start_states()
            weighted(0)
            for t in range(IT):
                if t % 2 == 1 and t < IT - 1:
                    split_2(pool, 15 + t // 2, True)
                if t % 4 == 0 and t // 4 + 1 < G:
                    weighted(t // 4 + 1)
                pool.wait_ge(S("y_sample"), t + 1)
                pool.dma_start(h_out[t], st[:, t % SB]).then_inc(S(f"so{t % SB}"), 16)
                if t + SB - 1 < IT:
                    if t >= 1:
                        pool.wait_ge(S(f"so{(t - 1) % SB}"), 16 * ((t - 1) // SB + 1))
                    state_in(t + SB - 1)
            split_2(pool, 22, True)
            pool.wait_ge(S("ncv_ready"), 1)
            pool.dma_start(o[3][0, 0], ncv[0:3, :]).then_inc(S("conv_out"), 16)
            pool.dma_start(o[5][0, :, 2, :], ncv[3:11, :]).then_inc(S("conv_out"), 16)
            for n in range(23, SSD_TILES):
                split_2(pool, n, True)
            for k in range(SB):
                pool.wait_ge(S(f"so{k}"), 16 * len(range(k, IT, SB)))
            pool.wait_ge(S("conv_out"), 48)
            pool.wait_ge(S("fin_out"), 16 * G)
            for n in range(SSD_TILES, ND + 2):
                split_2(pool, n, True)
            pool.wait_ge(S("v_out"), 16)
            pool.wait_ge(S("items_ready"), 1)
            n_items = pool.value_load(iti[0:1, ITEMS:ITEMS + 1], min_val=E, max_val=E + MORE)
            with pool.Fori(0, n_items) as item:
                for s_ in range(ETILES):
                    n = (s_ + 2) % ETILES
                    q, _ = eslot[n]
                    pool.wait_ge(S("part2"), item * ETILES + (ED + s_ + 2))
                    pool.wait_ge(S("part1"), item * ETILES + (ND + s_ + 2 + 1))
                    pool.tensor_tensor(part[:, n % PARTS, 1, SHARE:], raw_w[:, q, SHARE:],
                                       part[:, n % PARTS, 0, SHARE:].bitcast(F32),
                                       ALU.subtract).then_inc(S("part2_pool"), 1)

        @block.scalar
        def _(act):
            own = Order(act, S("act_own"))
            rows = [("norm_mix", 0, 0), ("norm_mix", 1, 8), ("norm_ffn", 0, 16), ("norm_ffn", 1, 24)]
            for name, row, at_ in rows:
                act.dma_start(vrow[at_:at_ + 8, 0, :], i[name][row].rearrange("(t p) -> t p", p=P)).then_inc(S("v_in"), 16)
            for src, at_, n in ((i["norm_final"], 32, 8), (i["ssd_gnorm"][0], 40, 16), (i["ssd_conv_b"][0], 56, 24),
                                (i["sgu_ln_g"][0], 80, 16), (i["sgu_ln_b"][0], 96, 16)):
                act.dma_start(vrow[at_:at_ + n, 0, :], src.rearrange("(t p) -> t p", p=P)).then_inc(S("v_in"), 16)
            act.dma_start(vrow[0:96, 1, :], i["ssd_conv_w"][0].rearrange("k (t p) -> (k t) p", p=P)).then_inc(S("v_in"), 16)
            act.dma_start(vrow[96:128, 1, :], i["sgu_b_in"][0].rearrange("(t p) -> t p", p=P)).then_inc(S("v_in"), 16)
            act.dma_start(crow, i["state_conv"][0].rearrange("b k n -> (b k) n")).then_inc(S("crow_in"), 16)
            act.dma_start(dtb, i["ssd_dt_bias"].rearrange("o h -> h o"), allow_slow_non_contiguous=True).then_inc(S("dtw_in"), 16)
            act.dma_start(alog, i["ssd_a_log"].rearrange("o h -> h o"), allow_slow_non_contiguous=True).then_inc(S("dtw_in"), 16)
            act.wait_ge(S("vec_tr"), 1)
            act.activation(V[:, :], psum[5][:, 0:240], ACT.Copy).then_inc(S("vec_ready"), 1)

            def norm(n, before_, ahead=lambda m: None):
                for m in range(DT):
                    ahead(m)
                    act.wait_ge(S("x_ready"), DT * n + m + 1)
                    if m >= 2 or n > 0:
                        act.wait_ge(S("sq_used"), DT * n + before_ + m - 1)
                    act.activation(sq[:, m % 2, :], xT[:, m, :], ACT.Square).then_inc(S("sq_ready"), 1)
                act.wait_ge(S("ms_ready"), n + 1)
                act.activation(rs[:, 1, :], rs[:, 0, :], ACT.Sqrt).then_inc(S("root_ready"), 1)
                if n < 3:
                    for m in nk:
                        act.wait_ge(S("a_ready"), DT * n + m + 1)
                        act.activation(ah[:, m, :], aT[:, m, :], ACT.Copy).then_inc(S("a1"), 1)

            split_1(act, 0)
            split_1(act, 1)
            norm(0, 0)
            act.wait_ge(S("dtw_in"), 32)
            act.activation(aneg, alog, ACT.Exp).then_inc(S("a_exp"), 1)
            for n in range(CT):
                if n % 2 == 0:
                    split_1(act, n // 2 + 2)
                act.wait_ge(S("proj"), n + 1)
                if n >= 2:
                    act.wait_ge(S("conv_done"), n - 1)
                if n == 0:
                    act.wait_ge(S("pads"), 2)
                    act.wait_ge(S("convS_ready"), 2)
                act.activation(raw[:, n % 2, 3:259], psum[n % 2][:, 0:NP_], ACT.Copy).then_inc(S("raw_ready"), 1)
                act.activation(convS[:, XO[n], :, 3], psum[n % 2][:, NP_:T], ACT.Copy).then_inc(S("raw_ready"), 1)
                if n == 4:
                    act.wait_ge(S("dt_abs"), 1)
                    own.did(act.activation(dtw, dtw, ACT.Exp, scale=-1.0))
                    own.settle()
                    act.activation(dtw, dtw, ACT.Ln, bias=1.0).then_inc(S("dt_log"), 1)
                if n == 8:
                    act.wait_ge(S("dsx_dt"), 1)
                    act.activation(dsx[:, 8:16], dsx[:, 8:16], ACT.Exp).then_inc(S("dsx_ready"), 1)
                    act.wait_ge(S("wend_in"), 1)
                    act.activation(wend, wend, ACT.Exp).then_inc(S("wend_ready"), 1)
                if n >= 1:
                    act.wait_ge(S("conv_done"), n)
                    t = XO[n - 1]
                    act.activation(xbc[:, t, :], xbc[:, t, :], ACT.Silu, bias=V[:, CB_ + t:CB_ + t + 1]).then_inc(S("xbc_ready"), 1)
                if n == 10:
                    for c in range(2):
                        act.wait_ge(S("misc"), c + 1)
                        act.activation(Btok[:, c, :], psum[5 + c][:, :], ACT.Copy).then_inc(S("misc_free"), 1)
                if n == 11:
                    for c in range(2):
                        act.wait_ge(S("misc"), c + 3)
                        act.activation(bcs[:, 512 * c:512 * c + 512], psum[5 + c][0:NS, :], ACT.Copy).then_inc(S("misc_free"), 1)
            act.wait_ge(S("conv_done"), CT)
            act.activation(xbc[:, 15, :], xbc[:, 15, :], ACT.Silu, bias=V[:, CB_ + 15:CB_ + 16]).then_inc(S("xbc_ready"), 1)

            fin_out = o[2][0, 0].rearrange("(g t w) q n -> g (w q) t n", g=G, w=2)
            misc = 4
            split_1(act, 14)
            for t in range(IT + 1):
                if t < IT:
                    act.wait_ge(S("seg_ready"), t + 1)
                    if t:
                        act.wait_ge(S("ce_ready"), t)
                    act.activation(el, psum[2 + t % 2][:, :].rearrange("p (h c i) -> p h c i", h=2, c=2)[:, :, 1, :],
                                   ACT.Exp).then_inc(S("el_ready"), 1)
                    if t:
                        act.wait_ge(S("m_ready"), t)
                    act.activation(ex, seg, ACT.Exp).then_inc(S("ex_ready"), 1)
                    if t % 4 == 0:
                        g = t // 4
                        act.wait_ge(S("misc"), misc + 1)
                        act.activation(hp, psum[5 + misc % 2][:, :], ACT.Copy).then_inc(S("misc_free"), 1)
                        misc += 1
                        act.wait_ge(S("misc"), misc + 1)
                        if g:
                            act.wait_ge(S("fin_out"), 16 * g)
                        act.activation(fin, psum[5 + misc % 2][:, :], ACT.Copy).then_inc(S("misc_free"), 1)
                        misc += 1
                        act.wait_ge(S("misc_free"), misc)
                        act.dma_start(fin_out[g], fin.rearrange("p (t n) -> p t n", t=4)).then_inc(S("fin_out"), 16)
                        if g:
                            act.wait_ge(S("y_sample"), t)
                        for w in range(2):
                            for half in range(2):
                                act.wait_ge(S("misc"), misc + 1)
                                act.activation(sbc[:, w, 4 * half:4 * half + 4, :],
                                               psum[5 + misc % 2][:, :].rearrange("p (b n) -> p b n", b=4),
                                               ACT.Copy).then_inc(S("misc_free"), 1)
                                misc += 1
                    act.wait_ge(S("proj"), CT + t + 1)
                    act.activation(zT[:, t, :], psum[(CT + t) % 2][:, 0:T], ACT.Copy).then_inc(S("z_ready"), 1)
                    if t % 2 == 1 and t < IT - 1:
                        split_1(act, 15 + t // 2)
                    act.wait_ge(S(f"st{t % SB}"), 16 * (t // SB + 1))
                    act.wait_ge(S("sexp_ready"), 2)
                    for b in range(NS):
                        n = NS * t + b
                        if n >= HB:
                            act.wait_ge(S("upd"), n - HB + 1)
                        act.activation(hd[:, n % HB, :], st[:, t % SB, b, :], ACT.Copy,
                                       scale=sexp[:, t, 1, b:b + 1]).then_inc(S("decayed"), 1)
            split_1(act, 22)
            act.wait_ge(S("z_ready"), IT)
            for g in range(G):
                act.activation(zT[:, 4 * g:4 * g + 4, :], zT[:, 4 * g:4 * g + 4, :], ACT.Silu).then_inc(S("gate_ready"), 1)
            for g in range(G):
                for k in range(4):
                    n = 4 * g + k
                    act.wait_ge(S("gated"), n + 1)
                    act.wait_ge(S("sq_used"), DT + n - 1)
                    act.activation(sq[:, n % 2, :], zT[:, n, :], ACT.Square).then_inc(S("sq_ready"), 1)
                for g_ in ([g - 1] if g else []) + ([g] if g == G - 1 else []):
                    act.wait_ge(S("gms_ready"), g_ + 1)
                    act.activation(rs[:, 1, :], rs[:, 0, :], ACT.Sqrt).then_inc(S("groot_ready"), 1)
                    for n in range(4 * g_, 4 * g_ + 4):
                        act.wait_ge(S("yg_ready"), n + 1)
                        act.activation(zh[:, n, :], zT[:, n, :], ACT.Copy).then_inc(S("yg1"), 1)
            norm(1, IT, lambda m: split_1(act, 22 + m) if m else None)
            act.dma_start(wsr, i["sgu_w_s"][0].rearrange("g i j -> i g j")).then_inc(S("ws_in"), 16)
            act.dma_start(bsr, i["sgu_b_s"][0]).then_inc(S("bs_in"), 16)
            act.wait_ge(S("fin_out"), 16 * G)
            for n in range(FT + 1):
                if n < FT:
                    split_1(act, SSD_TILES + n + 2)
                    act.wait_ge(S("ffn"), n + 1)
                    if n >= 2:
                        act.wait_ge(S("ffn_h"), n - 1)
                    act.activation(fs[:, n % 2, :], psum[2 * (n % 2)][:, 0:T], ACT.Silu).then_inc(S("ffn_silu"), 1)
                if n:
                    act.wait_ge(S("ffn_h"), n)
                    act.activation(hh[:, n - 1, :], hf[:, (n - 1) % 2, :], ACT.Copy).then_inc(S("ffn_h1"), 1)
            D0 = SSD_TILES + FT

            def ahead_down(m):
                split_1(act, D0 + 2 * m + 2)
                split_1(act, D0 + 2 * m + 3)

            norm(2, IT, ahead_down)
            U0 = D0 + 16
            for n in range(2 * IT):
                t = n % IT
                if n % 2 == 0:
                    split_1(act, U0 + n // 2 + 2)
                act.wait_ge(S("sgu"), n + 1)
                dst = (vT if n < IT else uT)[:, t, :]
                c = BI + (IT + t if n < IT else t)
                act.activation(dst, psum[n % 2][:, 0:T], ACT.Gelu, bias=V[:, c:c + 1]).then_inc(S("gelu"), 1)
                if n >= IT:
                    act.wait_ge(S("v_centred"), t + 1)
                    act.wait_ge(S("sq_used"), 3 * DT + IT + t - 1)
                    act.activation(sq[:, t % 2, :], vT[:, t, :], ACT.Square).then_inc(S("sq_ready"), 1)
            act.wait_ge(S("vms_ready"), 1)
            act.activation(rs[:, 1, :], rs[:, 0, :], ACT.Sqrt).then_inc(S("vroot_ready"), 1)
            for t in range(IT):
                act.wait_ge(S("gated_u"), t + 1)
                act.activation(uh[:, t, :], uT[:, t, :], ACT.Copy).then_inc(S("u1"), 1)
            act.wait_ge(S("vnew_ready"), 4)
            act.dma_start(o[6].rearrange("o b s d -> (o b s) d"), vnew).then_inc(S("v_out"), 16)
            act.wait_ge(S("u2"), IT)
            act.dma_start(wr, i["moe_w_router"][0].rearrange("(k p) e -> p k e", p=P)).then_inc(S("wr_in"), 16)
            norm(3, 2 * IT, lambda m: split_1(act, U0 + 16 + m + 2))
            act.wait_ge(S("diff_ready"), 1)
            act.activation(ed, ed, ACT.Exp).then_inc(S("ediff_ready"), 1)
            for half in range(2):
                act.wait_ge(S("m_mm"), half + 1)
                act.activation(xh[:, 4 * half:4 * half + 4, :].rearrange("p m c -> p (m c)"), psum[6 + half][:, :],
                               ACT.Copy).then_inc(S("m1"), 1)
            act.wait_ge(S("items_ready"), 1)
            n_items = act.value_load(iti[0:1, ITEMS:ITEMS + 1], min_val=E, max_val=E + MORE)
            with act.Fori(0, n_items) as item:
                def first_part(use, out):
                    act.wait_ge(S("m_mm"), item * USES + (2 + use + 1))
                    act.activation(out.rearrange("p m c -> p (m c)"), psum[6 + use % 2][:, :], ACT.Copy).then_inc(S("m1"), 1)

                for s_ in range(ETILES):
                    n = (s_ + 2) % ETILES
                    q, landed_ = eslot[n]
                    act.wait_ge(S(f"w{q}"), item * (ETILES // RING * 16) + (landed_ + (ETILES // RING * 16 if n < 2 else 0)))
                    act.wait_ge(S("w_used"), item * ETILES + (s_ + 1))
                    act.activation(part[:, n % PARTS, 0, :], raw_w[:, q, :], ACT.Copy).then_inc(S("part1"), 1)
                    if s_ % 4 == 0 and 4 <= s_ <= 28:
                        j = s_ // 4 - 1
                        if j >= 2:
                            act.wait_ge(S("e_h"), item * 7 + (j - 1))
                        act.activation(es[:, j % 2, :], psum[2 * (j % 2)][:, :], ACT.Silu).then_inc(S("e_silu"), 1)
                    if s_ % 4 == 0 and 8 <= s_ <= 28:
                        j = s_ // 4 - 2
                        first_part(HTR[j], hEh[:, 4 * j:4 * j + 4, :])
                    if s_ == 28:
                        for half in range(2):
                            first_part(GA + half, xh[:, 4 * half:4 * half + 4, :])
                    if s_ == 30:
                        first_part(HTR[6], hEh[:, 24:28, :])
                act.wait_ge(S("w_used"), item * ETILES + (ETILES + 1))
                for half in range(2):
                    act.activation(yt[:, 512 * half:512 * half + 512], psum[4 + half][:, :], ACT.Copy).then_inc(S("e_y"), 1)
            norm(4, 2 * IT)

        @block.tensor
        def _(pe):
            mm, tr = pe.matmul, pe.transpose
            pe.wait_ge(S("consts"), 3)
            pe.wait_ge(S("v_in"), 16 * 11)
            tr(psum[5][:, 0:112], vrow[0:112, 0, :], ident[0:112, 0:112])
            tr(psum[5][:, 112:240], vrow[:, 1, :], ident[:, :]).then_inc(S("vec_tr"), 1)
            pe.wait_ge(S("x_in"), 32)
            for m in nk:
                if m >= 2:
                    pe.wait_ge(S("x_ready"), m - 1)
                for n in range(3):
                    ins = tr(psum[m % 2][:, P * n:P * n + ROWS[n]], xtok[0:ROWS[n], n, P * m:P * m + P],
                             ident[0:ROWS[n], 0:ROWS[n]])
                ins.then_inc(S("x_tr"), 1)
            pe.wait_ge(S("crow_in"), 16)
            pe.wait_ge(S("vec_ready"), 1)
            for half in range(2):
                for t in range(12):
                    ins = tr(psum[5 + half][:, 24 * t:24 * t + 24], crow[:, P * (12 * half + t):P * (12 * half + t) + P],
                             ident[0:24, 0:24])
                ins.then_inc(S("crow_tr"), 1)

            def sum_square(n, before_, m):
                pe.wait_ge(S("sq_ready"), DT * n + before_ + m + 1)
                mm(psum[7][:, 0:T], ones[:, :], sq[:, m % 2, :], start=(m == 0), stop=(m == DT - 1)).then_inc(S("sq_used"), 1)

            def weight(n):
                _, kt, width = dense[n]
                split_done(pe, n)
                return [part[:, n % PARTS, u, 0:kt * width].rearrange("p (k n) -> p k n", k=kt) for u in range(2)]

            def product(out, w, x, start, stop):
                mm(out, w[0], x[0], start=start, stop=False)
                mm(out, w[1], x[0], start=False, stop=False)
                return mm(out, w[0], x[1], start=False, stop=stop)

            def dense_tile(bank, w, c, x, start=True, stop=True, k0=0, ready=lambda k: None):
                kt = w[0].shape[1]
                for k in range(kt):
                    ready(k)
                    ins = product(psum[bank][:, 0:T], [u[:, k, c:c + P] for u in w], [u[:, k0 + k, :] for u in x],
                                  start and k == 0, stop and k == kt - 1)
                return ins

            a12 = (ah, al)

            def normed(n, first):
                return lambda k: pe.wait_ge(S("a2"), DT * n + k + 1) if first else None

            for m in nk:
                sum_square(0, 0, m)
            pe.wait_ge(S("wdt_in"), 16)
            pe.wait_ge(S("convS_ready"), 2)
            for k in nk:
                pe.wait_ge(S("a_ready"), k + 1)
                ins = mm(psum[6][0:H, 0:T], wdt[:, k, :], aT[:, k, :], start=(k == 0), stop=(k == DT - 1))
            ins.then_inc(S("dt_mm"), 1)

            def xtr(q):
                pe.wait_ge(S("xbc_ready"), 8 + q + 1)
                if q >= 2:
                    pe.wait_ge(S("xdt_ready"), q - 1)
                for c in range(2):
                    ins = tr(psum[2 + q % 2][:, P * c:P * c + P], xbc[:, q, P * c:P * c + P], ident[:, :])
                ins.then_inc(S("xtr"), 1)

            for n in range(CT):
                if n % 2 == 0:
                    w = weight(n // 2)
                if n >= 2:
                    pe.wait_ge(S("raw_ready"), 2 * (n - 1))
                dense_tile(n % 2, w, P * (n % 2), a12, ready=normed(0, n == 0)).then_inc(S("proj"), 1)
                if n == 7:
                    pe.wait_ge(S("dt_ready"), 1)
                    for c in range(2):
                        tr(psum[6][:, H * c:H * c + H], dtT[:, P * c:P * c + P], ident[0:H, 0:H])
                    for c in range(2):
                        tr(psum[6][:, 64 + H * c:64 + H * c + H], LAT[:, P * c:P * c + P], ident[0:H, 0:H])
                    mm(psum[6][:, P:P + 64], ones[0:H, :], dle, start=True, stop=True).then_inc(S("dtk_tr"), 1)
                if n == 9:
                    pe.wait_ge(S("spread_ready"), 1)
                    mm(psum[6][:, 256:512], halves, dspr, start=True, stop=True).then_inc(S("sexp_mm"), 1)
                if n == 10:
                    pe.wait_ge(S("xbc_ready"), 8)
                    pe.wait_ge(S("sexp_ready"), 2)
                    for c in range(2):
                        for g in range(G):
                            ins = tr(psum[5 + c][:, P * g:P * g + P], xbc[:, 16 + g, P * c:P * c + P], ident[:, :])
                        ins.then_inc(S("misc"), 1)
                    for half in range(2):
                        for g in (2 * half, 2 * half + 1):
                            for c in range(2):
                                a = 256 * (g % 2) + P * c
                                ins = mm(psum[2 + half][:, a:a + P], xbc[:, 16 + g, P * c:P * c + P],
                                         xbc[:, 20 + g, P * c:P * c + P], start=True, stop=True)
                        ins.then_inc(S("cb"), 1)
                if n == 11:
                    for w_ in range(2):
                        pe.wait_ge(S("misc_free"), w_ + 1)
                        for g in range(G):
                            ins = tr(psum[5 + w_][0:NS, P * g:P * g + P], xbc[:, 16 + 4 * w_ + g, NP_:T], ident[:, :])
                        ins.then_inc(S("misc"), 1)
                    pe.wait_ge(S("cbm_ready"), 2)
                if n >= 12:
                    xtr(n - 12)
            for q in range(12, IT):
                xtr(q)

            def log_decay(t):
                if t >= 2:
                    pe.wait_ge(S("seg_ready"), t - 1)
                    pe.wait_ge(S("el_ready"), t - 1)
                if t == 0:
                    pe.wait_ge(S("xdt_ready"), IT)
                for h in range(2):
                    ins = mm(psum[2 + t % 2][:, 256 * h:256 * h + 256], col1(2 * t + h), LAT, start=True, stop=True)
                ins.then_inc(S("la"), 1)

            misc = 4
            log_decay(0)
            for t in range(IT + 1):
                if t + 1 < IT:
                    log_decay(t + 1)
                if t:
                    u = t - 1
                    pe.wait_ge(S("m_ready"), u + 1)
                    pe.wait_ge(S("ce_ready"), u + 1)
                    if u >= 1:
                        pe.wait_ge(S("y_done"), u)
                    if u % 4 == 0:
                        pe.wait_ge(S("misc_free"), 4 + 6 * (u // 4) + 1)
                    for h in range(2):
                        out = psum[4][64 * h:64 * h + 64, :]
                        xd = slice(P * u + 64 * h, P * u + 64 * h + 64)
                        mm(out[:, 0:P], Xdt[:, 0, xd], mm_[:, u % 2, h, 0, :], start=True, stop=True)
                        mm(out[:, P:2 * P], Xdt[:, 1, xd], mm_[:, u % 2, h, 1, :], start=True, stop=False)
                        hc = P * (u % 4) + 64 * h
                        ins = mm(out[:, P:2 * P], hp[:, hc:hc + 64], ce[:, u % 2, h, :], start=False, stop=True)
                    ins.then_inc(S("y_mm"), 1)
                if t < IT:
                    n = CT + t
                    if t % 2 == 0:
                        w = weight(n // 2)
                    if t >= 2:
                        pe.wait_ge(S("z_ready"), t - 1)
                    if t == 0:
                        pe.wait_ge(S("raw_ready"), 2 * CT)
                    dense_tile(n % 2, w, P * (n % 2), a12).then_inc(S("proj"), 1)
                if t < IT:
                    if t % 4 == 0:
                        g = t // 4
                        gs = slice(P * g, P * g + P)
                        pe.wait_ge(S("weighted"), 3 * g + 3)
                        pe.wait_ge(S("misc_free"), misc - 1)
                        mm(psum[5 + misc % 2][:, :], Btok[:, 0, gs], xsf[:, 0, :], start=True, stop=True).then_inc(S("misc"), 1)
                        misc += 1
                        pe.wait_ge(S("misc_free"), misc - 1)
                        for q in range(4):
                            for c in range(2):
                                ins = mm(psum[5 + misc % 2][:, P * q:P * q + P], xsf[:, 1 + c, P * q:P * q + P],
                                         Btok[:, c, gs], start=(c == 0), stop=(c == 1))
                        ins.then_inc(S("misc"), 1)
                        misc += 1
                        for w_ in range(2):
                            for half in range(2):
                                pe.wait_ge(S("misc_free"), misc - 1)
                                for b in range(4):
                                    ins = mm(psum[5 + misc % 2][:, P * b:P * b + P],
                                             ident[0:NS, 4 * half + b:4 * half + b + 1].to_broadcast((NS, P)),
                                             bcs[:, 512 * w_ + P * g:512 * w_ + P * g + P], start=True, stop=True)
                                ins.then_inc(S("misc"), 1)
                                misc += 1
            for g in range(G):
                if g >= 2:
                    pe.wait_ge(S("gms_ready"), g - 1)
                for k in range(4):
                    pe.wait_ge(S("sq_ready"), DT + 4 * g + k + 1)
                    mm(psum[(7, 4)[g % 2]][:, 0:T], ones[:, :], sq[:, k % 2, :], start=(k == 0), stop=(k == 3)
                       ).then_inc(S("sq_used"), 1)
                if g == 1:
                    pe.wait_ge(S("tail_ready"), 1)
                    for q in range(6):
                        pe.wait_ge(S("misc_free"), misc - (1 if q else 0))
                        for k in range(4):
                            ins = tr(psum[5 + misc % 2][0:11, P * k:P * k + P], tail[:, 4 * q + k, :], ident[:, :])
                        ins.then_inc(S("misc"), 1)
                        misc += 1

            def out_proj(n0, per, x, ready, n, before_):
                xbase = DT * n
                for m in nk:
                    if m >= 2:
                        pe.wait_ge(S("x_ready"), xbase + m - 1)
                    for c in range(per):
                        w = weight(n0 + per * m + c)
                        kt = w[0].shape[1]
                        ins = dense_tile(m % 2, w, 0, x, start=(c == 0), stop=(c == per - 1), k0=kt * c,
                                         ready=lambda k: pe.wait_ge(S(ready), kt * c + k + 1) if m == 0 else None)
                    ins.then_inc(S("o_mm"), 1)
                    if m:
                        sum_square(n, before_, m - 1)
                sum_square(n, before_, DT - 1)

            pe.wait_ge(S("z_ready"), IT)
            out_proj(20, 1, (zh, zl), "yg2", 1, IT)
            n0 = SSD_TILES
            for p in range(FT):
                w = weight(n0 + p)
                if p >= 2:
                    pe.wait_ge(S("ffn_h"), p - 1)
                for u in range(2):
                    ins = dense_tile(2 * (p % 2) + u, w, P * u, a12, ready=normed(1, p == 0 and u == 0))
                ins.then_inc(S("ffn"), 1)
            pe.wait_ge(S("ffn_h"), FT - 1)
            out_proj(n0 + FT, 2, (hh, hl), "ffn_h2", 2, IT)
            n0 += FT + 16
            pe.wait_ge(S("ws_in"), 16)
            for half in range(2):
                for g in range(4):
                    ins = tr(psum[4 + half][:, P * g:P * g + P], wsr[:, 4 * half + g, :], ident[:, :])
                ins.then_inc(S("ws_tr"), 1)

            def vtr(t):
                pe.wait_ge(S("vn_ready"), t + 1)
                if t >= 2:
                    pe.wait_ge(S("vtok_ready"), t - 1)
                for c in range(2):
                    ins = tr(psum[4 + t % 2][:, P * c:P * c + P], vT[:, t, P * c:P * c + P], ident[:, :])
                ins.then_inc(S("vtr"), 1)

            for n in range(2 * IT):
                if n % 2 == 0:
                    w = weight(n0 + n // 2)
                if n >= 2:
                    pe.wait_ge(S("gelu"), n - 1)
                dense_tile(n % 2, w, P * (n % 2), a12, ready=normed(2, n == 0)).then_inc(S("sgu"), 1)
                if 1 <= n <= IT:
                    pe.wait_ge(S("gelu"), n)
                    ins = mm(psum[7][:, 0:T], ones[:, :], vT[:, n - 1, :], start=(n == 1), stop=(n == IT))
                    if n == IT:
                        ins.then_inc(S("v_sum"), 1)
                if n >= IT + 1:
                    t = n - IT - 1
                    pe.wait_ge(S("sq_ready"), 3 * DT + IT + t + 1)
                    mm(psum[6][:, 0:T], ones[:, :], sq[:, t % 2, :], start=(t == 0), stop=False).then_inc(S("sq_used"), 1)
            pe.wait_ge(S("sq_ready"), 3 * DT + 2 * IT)
            mm(psum[6][:, 0:T], ones[:, :], sq[:, 1, :], start=False, stop=True).then_inc(S("sq_used"), 1)
            pe.wait_ge(S("wsT_ready"), 2)
            for t in range(IT):
                vtr(t)
            for q in range(4):
                if q:
                    pe.wait_ge(S("vnew_ready"), q)
                for k in range(4):
                    ins = tr(psum[6][0:NS, P * k:P * k + P], vT[:, 4 * q + k, NP_:T], ident[:, :])
                ins.then_inc(S("vnew_tr"), 1)
            pe.wait_ge(S("vtok_ready"), IT)
            pe.wait_ge(S("bs_in"), 16)
            pe.wait_ge(S("gelu"), 2 * IT)
            for t in range(IT):
                g = t // 2
                if t >= 2:
                    pe.wait_ge(S("sp_done"), t - 1)
                for c in range(2):
                    out = psum[2 + t % 2][:, P * c:P * c + P]
                    mm(out, vtok[:, c, P * t:P * t + P], wsT[:, g, :], start=True, stop=False)
                    ins = mm(out, ident[0:8, g:g + 1].to_broadcast((8, P)), bsr, start=False, stop=True)
                ins.then_inc(S("sp_mm"), 1)
            out_proj(n0 + 16, 1, (uh, ul), "u2", 3, 2 * IT)
            pe.wait_ge(S("wr_in"), 16)
            for n in range(3):
                for k in nk:
                    if n == 0:
                        pe.wait_ge(S("a_ready"), 3 * DT + k + 1)
                    ins = mm(psum[4][0:ROWS[n], 8 * n:8 * n + 8], aT[:, k, P * n:P * n + ROWS[n]], wr[:, k, :],
                             start=(k == 0), stop=(k == DT - 1))
            ins.then_inc(S("logits"), 1)
            for n in range(3):
                for half in range(2):
                    u = 2 * n + half
                    if u >= 2:
                        pe.wait_ge(S("atok_ready"), u - 1)
                    for k in range(4):
                        m = 4 * half + k
                        ins = tr(psum[half][0:ROWS[n], P * k:P * k + P], aT[:, m, P * n:P * n + ROWS[n]], ident[:, :])
                    ins.then_inc(S("atok_tr"), 1)
            pe.wait_ge(S("mask_ready"), 1)
            for n in range(4):
                for q in range(min(n + 1, 3)):
                    ins = mm(psum[5][:, 8 * n:8 * n + 8], (before if q == n else ones)[:, :], msk[:, q, :],
                             start=(q == 0), stop=(q == min(n, 2)))
            ins.then_inc(S("ranks"), 1)

            def gather(free):
                for half in range(2):
                    free(half)
                    for k in range(4):
                        m = 4 * half + k
                        for n in range(3):
                            ins = mm(psum[6 + (half + GA) % 2][:, CAP * k:CAP * k + CAP],
                                     atok[0:ROWS[n], n, P * m:P * m + P], Sm[0:ROWS[n], n, :],
                                     start=(n == 0), stop=(n == 2))
                    ins.then_inc(S("m_mm"), 1)

            def turn_gates(item):
                pe.wait_ge(S("m_free"), item * USES + (GATES + 1))
                for n in range(3):
                    ins = tr(psum[6 + GATES % 2][:, P * n:P * n + ROWS[n]], SG[0:ROWS[n], n, :], ident[0:ROWS[n], 0:ROWS[n]])
                ins.then_inc(S("m_mm"), 1)

            def spread(item, u0, m):
                u = u0 + m
                if m == 0:
                    pe.wait_ge(S("e_y"), item * 2 + 2)
                pe.wait_ge(S("m_free"), item * USES + max(u + 1, 2 + GATES + 1))
                mm(psum[6 + u % 2][:, 0:T], yt[:, P * m:P * m + P], GT, start=True, stop=True).then_inc(S("m_mm"), 1)

            pe.wait_ge(S("atok_ready"), 6)
            pe.nop().then_inc(S("w_used"), 1)
            pe.wait_ge(S("s_ready"), 1)
            for half in range(2):
                for k in range(4):
                    m = 4 * half + k
                    for n in range(3):
                        ins = mm(psum[6 + half][:, CAP * k:CAP * k + CAP], atok[0:ROWS[n], n, P * m:P * m + P],
                                 Sm[0:ROWS[n], n, :], start=(n == 0), stop=(n == 2))
                ins.then_inc(S("m_mm"), 1)
            pe.wait_ge(S("items_ready"), 1)
            n_items = pe.value_load(iti[0:1, ITEMS:ITEMS + 1], min_val=E, max_val=E + MORE)
            with pe.Fori(0, n_items) as item:
                def tile(s_):
                    pe.wait_ge(S("part2"), item * ETILES + (ED + s_ + 1))
                    pe.wait_ge(S("part2_pool"), item * ETILES + (ND + s_ + 1))
                    return [part[:, s_ % PARTS, u, :].rearrange("p (k n) -> p k n", k=4 if s_ < 28 else 2) for u in range(2)]

                def turn(j):
                    u = HTR[j]
                    pe.wait_ge(S("e_h"), item * 7 + (j + 1))
                    pe.wait_ge(S("m_free"), item * USES + (u + 1))
                    for k in range(4):
                        ins = tr(psum[6 + u % 2][:, P * k:P * k + P], hx[:, j % 2, P * k:P * k + P], ident[:, :])
                    ins.then_inc(S("m_mm"), 1)

                pe.wait_ge(S("x2"), item * 2 + 2)
                for j in range(7):
                    if j >= 2:
                        pe.wait_ge(S("e_h"), item * 7 + (j - 1))
                    for u in range(2):
                        for half in range(2):
                            w = tile(4 * j + 2 * u + half)
                            for k in range(4):
                                x = [v[:, 4 * half + k, :] for v in (xh, xl)]
                                out = psum[2 * (j % 2) + u][:, :]
                                mm(out, x[0], w[0][:, k, :], start=(half == 0 and k == 0), stop=False)
                                mm(out, x[0], w[1][:, k, :], start=False, stop=False)
                                ins = mm(out, x[1], w[0][:, k, :], start=False, stop=(half == 1 and k == 3))
                            ins.then_inc(S("w_used"), 1)
                            if j == 2:
                                spread(item, SP, 4 * u + 2 * half)
                                spread(item, SP, 4 * u + 2 * half + 1)
                    if j:
                        turn(j - 1)
                    else:
                        turn_gates(item)
                pe.wait_ge(S("s_ready"), item + 2)
                gather(lambda half: pe.wait_ge(S("m_free"), item * USES + (GA + half + 1)))
                for q in range(14):
                    w = tile(28 + q)
                    for kk in range(2):
                        kf = 2 * q + kk
                        if kf % 4 == 0:
                            pe.wait_ge(S("h2"), item * 7 + (kf // 4 + 1))
                        for half in range(2):
                            out = psum[4 + half][:, :]
                            c = slice(512 * half, 512 * half + 512)
                            mm(out, hEh[:, kf, :], w[0][:, kk, c], start=(kf == 0), stop=False)
                            mm(out, hEh[:, kf, :], w[1][:, kk, c], start=False, stop=False)
                            ins = mm(out, hEl[:, kf, :], w[0][:, kk, c], start=False, stop=(kf == ET - 1))
                    ins.then_inc(S("w_used"), 1)
                    if q == 1:
                        turn(6)
            turn_gates(n_items)
            for m in nk:
                spread(n_items, 1, m)
            for m in nk:
                sum_square(4, 2 * IT, m)
            for n in range(3):
                for half in range(2):
                    u = 2 * n + half
                    if u >= 2:
                        pe.wait_ge(S("yrow_ready"), u - 1)
                    for k in range(4):
                        m = 4 * half + k
                        if u < 2:
                            pe.wait_ge(S("a_ready"), 4 * DT + m + 1)
                        ins = tr(psum[half][0:ROWS[n], P * k:P * k + P], aT[:, m, P * n:P * n + ROWS[n]], ident[:, :])
                    ins.then_inc(S("yrow_tr"), 1)

        @block.vector
        def _(dve):
            own = Order(dve, S("dve_own"))
            tt, ts, stt = dve.tensor_tensor, dve.tensor_scalar, dve.scalar_tensor_tensor

            def step(ins):
                own.did(ins)
                own.settle()

            for m in nk:
                dve.wait_ge(S("x_tr"), m + 1)
                dve.tensor_copy(xT[:, m, :], psum[m % 2][:, 0:T]).then_inc(S("x_ready"), 1)
            dve.wait_ge(S("x_tr"), DT)
            dve.wait_ge(S("vec_ready"), 1)

            def inverse(root, bank, width):
                ts(rs[:, 0, :], psum[bank][:, 0:T], 1.0 / width, EPS, ALU.mult, ALU.add).then_inc(S(root[0]), 1)
                dve.wait_ge(S(root[1]), root[2])
                step(dve.reciprocal(rs[:, 0, :], rs[:, 1, :]))

            def norm(n, before_):
                dve.wait_ge(S("sq_used"), DT * (n + 1) + before_)
                inverse(("ms_ready", "root_ready", n + 1), 7, D)
                for m in range(DT + 1):
                    if m < DT:
                        c = NORM[n] + m
                        stt(out=aT[:, m, :], in0=xT[:, m, :], scalar=V[:, c:c + 1], in1=rs[:, 0, :],
                            op0=ALU.mult, op1=ALU.mult).then_inc(S("a_ready"), 1)
                    if m and n < 3:
                        dve.wait_ge(S("a1"), DT * n + m)
                        tt(al[:, m - 1, :], aT[:, m - 1, :], ah[:, m - 1, :].bitcast(F32), ALU.subtract).then_inc(S("a2"), 1)

            dve.memset(raw[:, 0, 0:3], 0.0).then_inc(S("pads"), 1)
            dve.memset(raw[:, 1, 0:3], 0.0).then_inc(S("pads"), 1)
            dve.wait_ge(S("pads"), 2)
            for half in range(2):
                dve.wait_ge(S("crow_tr"), half + 1)
                dve.tensor_copy(convS[:, 12 * half:12 * half + 12, :, 0:3],
                                psum[5 + half][:, 0:288].rearrange("p (t b k) -> p t b k", t=12, b=NS)
                                ).then_inc(S("convS_ready"), 1)
            dve.wait_ge(S("convS_ready"), 2)
            norm(0, 0)
            dve.wait_ge(S("vec_tr"), 1)
            dve.nop().then_inc(S("start_over"), 1)
            dve.wait_ge(S("dtw_in"), 32)
            dve.wait_ge(S("dt_mm"), 1)
            step(ts(dtT, psum[6][0:H, 0:T], dtb, None, ALU.add))
            step(stt(out=dtw, in0=dtT, scalar=-1.0, in1=dtT, op0=ALU.mult, op1=ALU.max))
            dve.nop().then_inc(S("dt_abs"), 1)
            dve.wait_ge(S("a_exp"), 1)
            step(ts(aneg, aneg, -1.0, None, ALU.mult))

            def conv(n):
                t = XO[n]
                dve.wait_ge(S("raw_ready"), 2 * n + 2)
                u = raw[:, n % 2, :]
                cw = [V[:, CW + CT * k + t:CW + CT * k + t + 1] for k in range(4)]
                out = xbc[:, t, 0:NP_]
                own.did(ts(cs1, u[:, 0:256], cw[0], None, ALU.mult))
                own.did(tt(cprod, convS[:, t],
                           V[:, CW + t:CW + t + 3 * CT + 1:CT].unsqueeze(1).to_broadcast((P, NS, 4)), ALU.mult))
                own.settle()
                own.did(stt(out=cs1, in0=u[:, 1:257], scalar=cw[1], in1=cs1, op0=ALU.mult, op1=ALU.add))
                own.did(dve.tensor_reduce(xbc[:, t, NP_:T], cprod, AX, ALU.add))
                own.settle()
                step(stt(out=cs1, in0=u[:, 2:258], scalar=cw[2], in1=cs1, op0=ALU.mult, op1=ALU.add))
                own.did(dve.tensor_copy(tail[:, t, 0:3], u[:, 256:259]))
                own.did(dve.tensor_copy(tail[:, t, 3:11], convS[:, t, :, 3]))
                own.did(stt(out=out, in0=u[:, 3:259], scalar=cw[3], in1=cs1, op0=ALU.mult, op1=ALU.add))
                own.settle()
                dve.nop().then_inc(S("conv_done"), 1)

            def xdt(q):
                dve.wait_ge(S("xtr"), q + 1)
                tt(Xdt[:, :, P * q:P * q + P].rearrange("p c (h d) -> p c h d", h=2),
                   psum[2 + q % 2][:, 0:256].rearrange("p (c h d) -> p c h d", c=2, h=2),
                   dtk_v[:, 0, :, 2 * q:2 * q + 2].unsqueeze(3).to_broadcast((P, 2, 2, 64)),
                   ALU.mult).then_inc(S("xdt_ready"), 1)

            for n in range(CT):
                if n >= 13:
                    xdt(n - 13)
                conv(n)
                if n == 4:
                    dve.wait_ge(S("dt_log"), 1)
                    step(stt(out=dtT, in0=dtT, scalar=0.0, in1=dtw, op0=ALU.max, op1=ALU.add))
                    own.did(ts(dtv, dtT, aneg, None, ALU.mult))
                    own.did(dve.memset(laraw, 1.0))
                    own.settle()
                    for c in range(2):
                        own.did(dve.tensor_tensor_scan(LAT[:, P * c:P * c + P], laraw[:, P * c:P * c + P],
                                                       dtv[:, P * c:P * c + P], 0.0, ALU.mult, ALU.add))
                    own.did(dve.tensor_copy(dsx[:, 0:8], dtT[:, NP_:T]))
                    own.did(dve.tensor_copy(dsx[:, 8:16], dtv[:, NP_:T]))
                    own.settle()
                    for c in range(2):
                        own.did(ts(dle[:, H * c:H * c + H], ident[0:H, 0:H], LAT[:, P * c + 127:P * c + 128], None, ALU.mult))
                    own.settle()
                    dve.nop().then_inc(S("dsx_dt"), 1)
                    dve.nop().then_inc(S("dt_ready"), 1)
                if n == 8:
                    dve.wait_ge(S("dtk_tr"), 1)
                    step(dve.tensor_copy(dtk, psum[6][:, 0:P]))
                    le = psum[6][:, P:P + 64]
                    own.did(tt(wend[:, 0, :], le[:, 0:H], dtk_v[:, 1, 0, :], ALU.subtract))
                    own.did(tt(wend[:, 2, :], le[:, H:2 * H], dtk_v[:, 1, 1, :], ALU.subtract))
                    own.settle()
                    step(tt(wend[:, 1, :], le[:, H:2 * H], wend[:, 0, :], ALU.add))
                    dve.nop().then_inc(S("dtk_ready"), 1)
                    dve.nop().then_inc(S("wend_in"), 1)
                    idh = ident[0:H, 0:H]
                    own.did(dve.tensor_reduce(hsel, idh.rearrange("p (t w) -> p w t", w=2), AX, ALU.add))
                    own.did(dve.tensor_reduce(psel, idh.rearrange("p (t w) -> p t w", w=2), AX, ALU.add))
                    own.settle()
                    own.did(dve.tensor_copy(halves.rearrange("p (w q) -> p w q", w=2),
                                            hsel.unsqueeze(2).to_broadcast((H, 2, 64))))
                    dve.wait_ge(S("dsx_ready"), 1)
                    own.did(tt(dspr.rearrange("p (t n) -> p t n", t=IT), dsx.unsqueeze(1).to_broadcast((H, IT, 16)),
                               psel.unsqueeze(2).to_broadcast((H, IT, 16)), ALU.mult))
                    own.settle()
                    dve.nop().then_inc(S("spread_ready"), 1)
                if n == 9:
                    dve.wait_ge(S("sexp_mm"), 1)
                    dve.tensor_copy(sexp, psum[6][:, 256:512].rearrange("p (t w b) -> p t w b", t=IT, w=2)
                                    ).then_inc(S("sexp_ready"), 1)
                    dve.nop().then_inc(S("sexp_ready"), 1)
                if n == 10:
                    for half in range(2):
                        dve.wait_ge(S("cb"), half + 1)
                        tt(CBm[:, 2 * half:2 * half + 2].rearrange("p g c i -> p (g c) i"),
                           psum[2 + half][:, :].rearrange("p (a i) -> p a i", a=4),
                           causal[:, :].unsqueeze(1).to_broadcast((P, 4, P)), ALU.mult).then_inc(S("cbm_ready"), 1)
            dve.nop().then_inc(S("tail_ready"), 1)
            for q in range(11, IT):
                xdt(q)
            dve.wait_ge(S("xbc_ready"), CT)
            dve.wait_ge(S("sexp_ready"), 2)
            step(tt(dtx, xbc[:, 0:IT, NP_:T], sexp[:, :, 0, :], ALU.mult))
            dve.wait_ge(S("cols_in"), 64)
            dve.wait_ge(S("cbm_ready"), 2)

            def y_out(u):
                dve.wait_ge(S("y_mm"), u + 1)
                stt(out=xbc[:, u, 0:NP_], in0=xbc[:, u, 0:NP_], scalar=dcol[:, u:u + 1], in1=psum[4][:, 0:256],
                    op0=ALU.mult, op1=ALU.add).then_inc(S("y_done"), 1)

            def segments(t):
                dve.wait_ge(S("la"), t + 1)
                if t:
                    dve.wait_ge(S("m_ready"), t)
                la = psum[2 + t % 2][:, :].rearrange("p (h c i) -> p h c i", h=2, c=2)
                for h in range(2):
                    for c in range(2):
                        k = 2 * t + h
                        own.did(ts(seg[:, h, c, :], la[:, h, c, :], dtk_v[:, 1, c, k:k + 1], 0.0, ALU.subtract, ALU.min))
                own.settle()
                dve.nop().then_inc(S("seg_ready"), 1)

            segments(0)
            for t in range(IT):
                g = t // 4
                dve.wait_ge(S("el_ready"), t + 1)
                if t >= 2:
                    dve.wait_ge(S("y_mm"), t - 1)
                tt(ce[:, t % 2], el, xbc[:, 20 + g, P:2 * P].unsqueeze(1).to_broadcast((P, 2, P)),
                   ALU.mult).then_inc(S("ce_ready"), 1)
                dve.wait_ge(S("ex_ready"), t + 1)
                tt(mm_[:, t % 2].rearrange("p h c i -> p h (c i)"), ex.rearrange("p h c i -> p h (c i)"),
                   CBm[:, g].rearrange("p c i -> p (c i)").unsqueeze(1).to_broadcast((P, 2, 256)),
                   ALU.mult).then_inc(S("m_ready"), 1)
                if t + 1 < IT:
                    segments(t + 1)
                if t:
                    y_out(t - 1)
                if t % 4 == 0:
                    dve.wait_ge(S("misc_free"), 4 + 6 * g + 6)
                for b in range(NS):
                    n = NS * t + b
                    dve.wait_ge(S("decayed"), n + 1)
                    stt(out=st[:, t % SB, b, :], in0=sbc[:, 0, b, :], scalar=dtx[:, t, b:b + 1], in1=hd[:, n % HB, :],
                        op0=ALU.mult, op1=ALU.add).then_inc(S("upd"), 1)
                for b in range(NS):
                    dve.wait_ge(S("upd"), NS * t + b + 1)
                    own.settle(1)
                    own.did(dve.tensor_tensor_reduce(junk[:, b % 2], st[:, t % SB, b, :], sbc[:, 1, b, :], 1.0, 0.0,
                                                     ALU.mult, ALU.add, ys[:, b:b + 1]))
                own.settle()
                step(stt(out=xbc[:, t, NP_:T], in0=xbc[:, t, NP_:T], scalar=dcol[:, t:t + 1], in1=ys,
                         op0=ALU.mult, op1=ALU.add))
                dve.nop().then_inc(S("y_sample"), 1)
            y_out(IT - 1)
            dve.wait_ge(S("y_done"), IT)
            for t in range(IT):
                dve.wait_ge(S("gate_ready"), t // 4 + 1)
                tt(zT[:, t, :], zT[:, t, :], xbc[:, t, :], ALU.mult).then_inc(S("gated"), 1)
            for g in range(G + 1):
                if g < G:
                    dve.wait_ge(S("sq_used"), DT + 4 * g + 4)
                    if g:
                        dve.wait_ge(S("yg_ready"), 4 * g)
                    inverse(("gms_ready", "groot_ready", g + 1), (7, 4)[g % 2], DI // G)
                    for n in range(4 * g, 4 * g + 4):
                        stt(out=zT[:, n, :], in0=zT[:, n, :], scalar=V[:, GN + n:GN + n + 1], in1=rs[:, 0, :],
                            op0=ALU.mult, op1=ALU.mult).then_inc(S("yg_ready"), 1)
                for n in range(4 * g - 4, 4 * g):
                    if n >= 0:
                        dve.wait_ge(S("yg1"), n + 1)
                        tt(zl[:, n, :], zT[:, n, :], zh[:, n, :].bitcast(F32), ALU.subtract).then_inc(S("yg2"), 1)
                if g == 0:
                    for q in range(6):
                        u = 28 + q
                        dve.wait_ge(S("misc"), u + 1)
                        dve.tensor_copy(ncv[:, 512 * q:512 * q + 512], psum[5 + u % 2][0:11, :]).then_inc(S("misc_free"), 1)
                    dve.wait_ge(S("misc_free"), 34)
                    dve.nop().then_inc(S("ncv_ready"), 1)
            dve.nop().then_inc(S("ssd_over"), 1)

            def residual(n, ahead):
                for m in nk:
                    ahead(m)
                    dve.wait_ge(S("o_mm"), DT * (n - 1) + m + 1)
                    tt(xT[:, m, :], xT[:, m, :], psum[m % 2][:, 0:T], ALU.add).then_inc(S("x_ready"), 1)
                dve.wait_ge(S("x_ready"), DT * (n + 1))

            residual(1, lambda m: split_2(dve, 22 + m) if 22 + m >= SSD_TILES else None)
            norm(1, IT)
            dve.wait_ge(S("fin_out"), 16 * G)
            for n in range(FT + 1):
                if n < FT:
                    split_2(dve, SSD_TILES + n + 2)
                    dve.wait_ge(S("ffn_silu"), n + 1)
                    if n >= 2:
                        dve.wait_ge(S("ffn_h2"), n - 1)
                    tt(hf[:, n % 2, :], fs[:, n % 2, :], psum[2 * (n % 2) + 1][:, 0:T], ALU.mult).then_inc(S("ffn_h"), 1)
                if n:
                    dve.wait_ge(S("ffn_h1"), n)
                    tt(hl[:, n - 1, :], hf[:, (n - 1) % 2, :], hh[:, n - 1, :].bitcast(F32), ALU.subtract).then_inc(S("ffn_h2"), 1)
            D0 = SSD_TILES + FT

            def ahead_down(m):
                split_2(dve, D0 + 2 * m + 2)
                split_2(dve, D0 + 2 * m + 3)

            residual(2, ahead_down)
            norm(2, IT)
            U0 = D0 + 16
            for half in range(2):
                dve.wait_ge(S("ws_tr"), half + 1)
                tt(wsT[:, 4 * half:4 * half + 4, :], psum[4 + half][:, :].rearrange("p (g i) -> p g i", g=4),
                   causal[:, :].unsqueeze(1).to_broadcast((P, 4, P)), ALU.mult).then_inc(S("wsT_ready"), 1)
            for n in range(0, IT + 2, 2):
                split_2(dve, U0 + n // 2 + 2)
            dve.wait_ge(S("v_sum"), 1)
            step(ts(mus, psum[7][:, 0:T], -1.0 / DI, None, ALU.mult))
            for t in range(IT):
                dve.wait_ge(S("gelu"), t + 1)
                tt(vT[:, t, :], vT[:, t, :], mus, ALU.add).then_inc(S("v_centred"), 1)
                if t % 2 == 1 and t < IT - 1:
                    split_2(dve, U0 + (IT + t + 1) // 2 + 2)
            dve.wait_ge(S("v_centred"), IT)
            dve.wait_ge(S("sq_used"), 3 * DT + 2 * IT)
            inverse(("vms_ready", "vroot_ready", 1), 6, DI)
            for t in range(IT):
                own.did(stt(out=vT[:, t, :], in0=vT[:, t, :], scalar=V[:, LG + t:LG + t + 1], in1=rs[:, 0, :],
                            op0=ALU.mult, op1=ALU.mult))
                own.settle()
                ts(vT[:, t, :], vT[:, t, :], V[:, LB + t:LB + t + 1], None, ALU.add).then_inc(S("vn_ready"), 1)
                if t:
                    dve.wait_ge(S("vtr"), t)
                    dve.tensor_copy(vtok[:, :, P * (t - 1):P * t],
                                    psum[4 + (t - 1) % 2][:, 0:256].rearrange("p (c d) -> p c d", c=2)).then_inc(S("vtok_ready"), 1)
            dve.wait_ge(S("vtr"), IT)
            dve.tensor_copy(vtok[:, :, P * 15:P * 16],
                            psum[5][:, 0:256].rearrange("p (c d) -> p c d", c=2)).then_inc(S("vtok_ready"), 1)
            for q in range(4):
                dve.wait_ge(S("vnew_tr"), q + 1)
                dve.tensor_copy(vnew[:, 512 * q:512 * q + 512], psum[6][0:NS, :]).then_inc(S("vnew_ready"), 1)
            dve.wait_ge(S("gelu"), 2 * IT)
            for t in range(IT + 1):
                if t < IT:
                    g = t // 2
                    dve.wait_ge(S("vn_ready"), t + 1)
                    if t >= 2:
                        dve.wait_ge(S("ssm_used"), t - 1)
                    own.did(ts(ssm[:, t % 2, :], vT[:, t, NP_:T], w00[:, g:g + 1], b00[:, g:g + 1], ALU.mult, ALU.add))
                    dve.wait_ge(S("sp_mm"), t + 1)
                    tt(uT[:, t, 0:NP_], uT[:, t, 0:NP_], psum[2 + t % 2][:, 0:256], ALU.mult).then_inc(S("sp_done"), 1)
                    own.settle()
                    tt(uT[:, t, NP_:T], uT[:, t, NP_:T], ssm[:, t % 2, :], ALU.mult).then_inc(S("ssm_used"), 1)
                    dve.wait_ge(S("sp_done"), t + 1)
                    dve.wait_ge(S("ssm_used"), t + 1)
                    dve.nop().then_inc(S("gated_u"), 1)
                if t:
                    dve.wait_ge(S("u1"), t)
                    tt(ul[:, t - 1, :], uT[:, t - 1, :], uh[:, t - 1, :].bitcast(F32), ALU.subtract).then_inc(S("u2"), 1)
            dve.wait_ge(S("v_out"), 16)
            residual(3, lambda m: split_2(dve, U0 + 16 + m + 2))
            norm(3, 2 * IT)

            dve.wait_ge(S("iota"), 1)
            own.did(dve.tensor_copy(iota, ioti[:, :]))
            own.did(dve.memset(L, 0.0))
            own.did(dve.memset(valid, 1.0))
            own.did(dve.memset(SG, 0.0))
            own.did(dve.memset(incl, 1.0))
            own.settle()
            own.did(dve.memset(valid[:, 2:3], 0.0))
            own.did(ts(rev, iota[:, 0:E], -1.0, float(E), ALU.mult, ALU.add))
            for k in range(MORE // E):
                own.did(dve.tensor_copy(ev[:, E * k:E * k + E], iota[:, 0:E]))
            dve.wait_ge(S("logits"), 1)
            own.did(dve.tensor_copy(L[:, 0:2, :], psum[4][:, 0:16].rearrange("p (n e) -> p n e", n=2)))
            own.did(dve.tensor_copy(L[0:NS, 2, :], psum[4][0:NS, 16:24]))
            own.settle()
            step(dve.memset(valid[0:NS, 2:3], 1.0))
            wide = (P, 3, E)

            def first_max(src, m, oh):
                step(dve.tensor_reduce(m, src, AX, ALU.max))
                step(tt(eq, src, m.unsqueeze(2).to_broadcast(wide), ALU.is_equal))
                step(tt(eq, eq, rev.unsqueeze(1).to_broadcast(wide), ALU.mult))
                step(dve.tensor_reduce(mx, eq, AX, ALU.max))
                step(tt(oh, eq, mx.unsqueeze(2).to_broadcast(wide), ALU.is_equal))

            first_max(L, m1, oh1)
            step(stt(out=L2, in0=oh1, scalar=-3.0e38, in1=L, op0=ALU.mult, op1=ALU.add))
            first_max(L2, m2, oh2)
            own.did(tt(ed, m2, m1, ALU.subtract))
            own.did(tt(msk, oh1, oh2, ALU.add))
            own.settle()
            dve.nop().then_inc(S("diff_ready"), 1)
            step(tt(msk, msk, valid.unsqueeze(2).to_broadcast(wide), ALU.mult))
            dve.nop().then_inc(S("mask_ready"), 1)
            for u in range(6):
                n, half = u // 2, u % 2
                dve.wait_ge(S("atok_tr"), u + 1)
                dve.tensor_copy(atok[0:ROWS[n], n, 512 * half:512 * half + 512], psum[half][0:ROWS[n], :]).then_inc(S("atok_ready"), 1)
            dve.wait_ge(S("ediff_ready"), 1)
            step(ts(den, ed, 1.0, None, ALU.add))
            step(dve.reciprocal(g1, den))
            step(tt(g2, ed, g1, ALU.mult))
            own.did(tt(gw, oh1, g1.unsqueeze(2).to_broadcast(wide), ALU.mult))
            own.did(tt(eq, oh2, g2.unsqueeze(2).to_broadcast(wide), ALU.mult))
            own.settle()
            step(tt(gw, gw, eq, ALU.add))
            for k in range(MORE // E):
                own.did(dve.tensor_copy(gw2[:, :, E * k:E * k + E], gw))
            own.did(dve.tensor_copy(Gall[:, :, 0:E], gw))
            dve.wait_ge(S("ranks"), 1)
            rk = psum[5][:, 0:24].rearrange("p (n e) -> p n e", n=3)
            for k in range(CHUNKS):
                step(ts(pos, rk, FAR - CAP * k, None, ALU.add))
                step(tt(pos, pos, msk, ALU.mult))
                step(ts(Q[:, :, E * k:E * k + E], pos, -FAR, None, ALU.add))
            own.did(dve.tensor_copy(Aall[:, :, 0:E], Q[:, :, 0:E]))
            for k in range(1, CHUNKS):
                own.did(ts(pres[:, E * (k - 1):E * k], psum[5][:, 24:32], float(CAP * k) + 0.5, None, ALU.is_gt))
            own.settle()

            def chosen(j):
                for n in range(3):
                    own.did(ts(Sm[:, n, :], iota, Aall[:, n, bass.ds(j, 1)], None, ALU.is_equal))

            chosen(0)
            own.settle()
            dve.nop().then_inc(S("s_ready"), 1)
            step(dve.tensor_tensor_scan(OX[:, 0, :], incl, pres, float(E), ALU.mult, ALU.add))
            own.did(tt(incl, OX[:, 0, :], pres, ALU.mult))
            own.did(dve.tensor_copy(iti[0:1, ITEMS:ITEMS + 1], OX[0:1, 0, MORE - 1:MORE]))
            own.settle()
            step(ts(incl, incl, -1.0, None, ALU.add))
            jw = (P, MORE + 1, MORE)
            step(tt(OJ, iota[:, E:E + MORE + 1].unsqueeze(2).to_broadcast(jw), incl.unsqueeze(1).to_broadcast(jw), ALU.is_equal))
            own.did(dve.tensor_copy(itf[:, 0:E], iota[:, 0:E]))
            for src, dst in [(ev, itf[:, E:ITEMS])] + [(Q[:, n, E:E + MORE], Aall[:, n, E:ITEMS]) for n in range(3)] \
                    + [(gw2[:, n, :], Gall[:, n, E:ITEMS]) for n in range(3)]:
                step(tt(OX, OJ, src.unsqueeze(1).to_broadcast(jw), ALU.mult))
                step(dve.tensor_reduce(dst, OX, AX, ALU.add))
            step(dve.tensor_copy(iti[0:1, 0:ITEMS], itf[0:1, :]))
            own.did(dve.memset(yt, 0.0))
            own.settle()
            dve.nop().then_inc(S("e_y"), 2)
            dve.nop().then_inc(S("items_ready"), 1)
            n_items = dve.value_load(iti[0:1, ITEMS:ITEMS + 1], min_val=E, max_val=E + MORE)

            for half in range(2):
                dve.wait_ge(S("m1"), half + 1)
                tt(xl[:, 4 * half:4 * half + 4, :].rearrange("p m c -> p (m c)"), psum[6 + half][:, :],
                   xh[:, 4 * half:4 * half + 4, :].rearrange("p m c -> p (m c)").bitcast(F32),
                   ALU.subtract).then_inc(S("x2"), 1)
            dve.wait_ge(S("x2"), 2)
            dve.nop().then_inc(S("m_free"), 2)

            def take_gates(item):
                dve.wait_ge(S("m_mm"), item * USES + (2 + GATES + 1))
                dve.tensor_copy(GT, psum[6 + GATES % 2][:, 0:T]).then_inc(S("m_free"), 1)

            def spread(item, u0, m):
                u = u0 + m
                dve.wait_ge(S("m_mm"), item * USES + (2 + u + 1))
                tt(xT[:, m, :], xT[:, m, :], psum[6 + u % 2][:, 0:T], ALU.add).then_inc(S("m_free"), 1)

            before_loop = own.n
            STEPS = 6 + 9
            with dve.Fori(0, n_items) as item:
                own.base, own.n = item * STEPS + before_loop, 0

                def second_part(use, nth, out, first, sem):
                    dve.wait_ge(S("m1"), item * 9 + (2 + nth + 1))
                    own.did(tt(out.rearrange("p m c -> p (m c)"), psum[6 + use % 2][:, :],
                               first.rearrange("p m c -> p (m c)").bitcast(F32), ALU.subtract))
                    own.settle()
                    dve.nop().then_inc(S("m_free"), 1)
                    dve.nop().then_inc(S(sem), 1)

                for s_ in range(ETILES):
                    n = (s_ + 2) % ETILES
                    q, _ = eslot[n]
                    if s_ == 4:
                        take_gates(item)
                    if 9 <= s_ <= 12:
                        spread(item, SP, 2 * (s_ - 9))
                        spread(item, SP, 2 * (s_ - 9) + 1)
                    dve.wait_ge(S("part1"), item * ETILES + (ND + s_ + 2 + 1))
                    tt(part[:, n % PARTS, 1, 0:SHARE], raw_w[:, q, 0:SHARE], part[:, n % PARTS, 0, 0:SHARE].bitcast(F32),
                       ALU.subtract).then_inc(S("part2"), 1)
                    if s_ % 4 == 0 and 4 <= s_ <= 28:
                        j = s_ // 4 - 1
                        dve.wait_ge(S("e_silu"), item * 7 + (j + 1))
                        tt(hx[:, j % 2, :], es[:, j % 2, :], psum[2 * (j % 2) + 1][:, :], ALU.mult).then_inc(S("e_h"), 1)
                    if s_ % 4 == 0 and 8 <= s_ <= 28:
                        j = s_ // 4 - 2
                        second_part(HTR[j], j, hEl[:, 4 * j:4 * j + 4, :], hEh[:, 4 * j:4 * j + 4, :], "h2")
                    if s_ == 14:
                        for n in range(3):
                            own.did(ts(SG[:, n, :], iota, Aall[:, n, bass.ds(item, 1)],
                                       Gall[:, n, bass.ds(item, 1)], ALU.is_equal, ALU.mult))
                        chosen(item + 1)
                        own.settle()
                        dve.nop().then_inc(S("s_ready"), 1)
                    if s_ == 28:
                        for half in range(2):
                            c = slice(4 * half, 4 * half + 4)
                            second_part(GA + half, 6 + half, xl[:, c, :], xh[:, c, :], "x2")
                    if s_ == 30:
                        second_part(HTR[6], 8, hEl[:, 24:28, :], hEh[:, 24:28, :], "h2")
                assert own.n == STEPS, own.n
            take_gates(n_items)
            for m in nk:
                spread(n_items, 1, m)
            dve.wait_ge(S("m_free"), n_items * USES + (2 + 9))
            dve.nop().then_inc(S("x_ready"), DT)
            norm(4, 2 * IT)
            for u in range(6):
                n, half = u // 2, u % 2
                dve.wait_ge(S("yrow_tr"), u + 1)
                dve.tensor_copy(yrow[0:ROWS[n], n, 512 * half:512 * half + 512], psum[half][0:ROWS[n], :]).then_inc(S("yrow_ready"), 1)
            dve.wait_ge(S("yrow_ready"), 6)
            dve.nop().then_inc(S("y_stored"), 1)


_OUTS = [(1, 256, 1024), (8, 1, 1024), (1, 1, 32, 64, 128), (1, 1, 3, 3072), (1, 8, 32, 64, 128), (1, 8, 3, 3072), (1, 8, 1, 2048)]
_INS = ["x_prompt", "x_sample", "state_ssm", "state_conv", "norm_mix", "norm_ffn", "norm_final",
        "ssd_w_in", "ssd_conv_w", "ssd_conv_b", "ssd_dt_bias", "ssd_a_log", "ssd_d", "ssd_gnorm", "ssd_w_out",
        "sgu_w_in", "sgu_b_in", "sgu_ln_g", "sgu_ln_b", "sgu_w_s", "sgu_b_s", "sgu_w_out",
        "ffn_w_gu", "ffn_w_down", "moe_w_router", "moe_w_gu", "moe_w_down"]


def kernel(**inputs):
    import numpy as _np
    import concourse.bacc as _bacc
    from concourse import mybir as _mybir
    from concourse.bass_utils import run_bass_kernel_spmd as _run

    nc = _bacc.Bacc("TRN2", target_bir_lowering=False, num_devices=1)
    arrays, ins = {}, {}
    for name in _INS:
        a = _np.ascontiguousarray(inputs[name])
        arrays[f"in_{name}_dram"] = a
        ins[name] = nc.dram_tensor(f"in_{name}_dram", a.shape, _mybir.dt.from_np(a.dtype), kind="ExternalInput").ap()
    outs = [nc.dram_tensor(f"out_{n}_dram", s, _mybir.dt.float32, kind="ExternalOutput").ap() for n, s in enumerate(_OUTS)]
    hybrid_step(nc, ins, outs)
    r = _run(nc, [arrays], core_ids=[0])
    return tuple(r.results[0][f"out_{n}_dram"] for n in range(len(_OUTS)))
```
